# Optimizing a Trainium2 kernel written in Bass

```python
import jax, jax.numpy as jnp
from jax import lax
import numpy as np

D_MODEL = 1024
BATCH = 1
SEQ = 512
DEPTH = 2

CHUNK = 64
N_MIXERS = 2
POOL_WINDOWS = (2, 4, 8, 16)
N_POOL_GROUPS = len(POOL_WINDOWS)
POOL_GROUP_DIM = D_MODEL // N_POOL_GROUPS
CONV_WIDTH = 3
D_FF = ((8 * D_MODEL // 3 + 255) // 256) * 256
N_SUB = 3
N_MOD = 3
RMS_EPS = 1e-6
N_POOL_LAYERS = (DEPTH + 1) // 2
N_CONV_LAYERS = DEPTH // 2


def rms_norm(x, g):
    xf = x.astype(jnp.float32)
    y = xf * lax.rsqrt(jnp.mean(xf * xf, axis=-1, keepdims=True) + RMS_EPS)
    return (y * g.astype(jnp.float32)).astype(x.dtype)

def modulate(h, shift, scale):
    return h * (1 + scale[:, None, :]) + shift[:, None, :]

def swiglu(h, w_in, w_out):
    a, b = jnp.split(h @ w_in, 2, axis=-1)
    return (jax.nn.silu(a) * b) @ w_out

def pool_mixer(h, w_grp, scale):
    B, T, D = h.shape
    hg = h.reshape(B, T, N_POOL_GROUPS, POOL_GROUP_DIM)
    cs = jnp.cumsum(hg.astype(jnp.float32), axis=1)
    pos = jnp.arange(1, T + 1, dtype=jnp.float32)
    pooled = []
    for g, w in enumerate(POOL_WINDOWS):
        csg = cs[:, :, g]
        lag = jnp.pad(csg, ((0, 0), (w, 0), (0, 0)))[:, :T]
        cnt = jnp.minimum(pos, float(w))[None, :, None]
        pooled.append((csg - lag) / cnt)
    pooled = jnp.stack(pooled, axis=2).astype(h.dtype)
    mixed = pooled - hg
    y = jnp.einsum('btgc,gcd->btgd', mixed, w_grp).reshape(B, T, D)
    return y * scale

def conv_mixer(h, w_in, w_conv, w_out):
    D = h.shape[-1]
    b_gate, c_gate, v = jnp.split(h @ w_in, 3, axis=-1)
    u = c_gate * v
    conv = lax.conv_general_dilated(
        u, w_conv[:, None, :].astype(u.dtype),
        window_strides=(1,),
        padding=[(CONV_WIDTH - 1, 0)],
        dimension_numbers=('NWC', 'WIO', 'NWC'),
        feature_group_count=D)
    return (b_gate * conv) @ w_out

def first_inputs(seed: int = 0) -> dict:
    key = jax.random.key(seed)
    ks = jax.random.split(key, 14)
    f32 = jnp.float32
    x = jax.random.normal(ks[0], (BATCH, SEQ, D_MODEL), f32)
    c = jax.random.normal(ks[1], (BATCH, D_MODEL), f32)
    ada_w = jax.random.normal(ks[2], (DEPTH, D_MODEL, N_SUB * N_MOD * D_MODEL), f32) * D_MODEL ** -0.5
    ada_b = 0.01 * jax.random.normal(ks[3], (DEPTH, N_SUB * N_MOD * D_MODEL), f32)
    norm_g = 1.0 + 0.1 * jax.random.normal(ks[4], (DEPTH, N_SUB, D_MODEL), f32)
    ffn_w_in = jax.random.normal(ks[5], (DEPTH, 2, D_MODEL, 2 * D_FF), f32) * D_MODEL ** -0.5
    ffn_w_out = jax.random.normal(ks[6], (DEPTH, 2, D_FF, D_MODEL), f32) * D_FF ** -0.5
    pool_w = jax.random.normal(ks[7], (N_POOL_LAYERS, N_POOL_GROUPS, POOL_GROUP_DIM, POOL_GROUP_DIM), f32) * POOL_GROUP_DIM ** -0.5
    pool_scale = 1.0 + 0.1 * jax.random.normal(ks[8], (N_POOL_LAYERS, D_MODEL), f32)
    conv_w_in = jax.random.normal(ks[9], (N_CONV_LAYERS, D_MODEL, 3 * D_MODEL), f32) * D_MODEL ** -0.5
    conv_w = jax.random.normal(ks[10], (N_CONV_LAYERS, CONV_WIDTH, D_MODEL), f32) * CONV_WIDTH ** -0.5
    conv_w_out = jax.random.normal(ks[11], (N_CONV_LAYERS, D_MODEL, D_MODEL), f32) * D_MODEL ** -0.5
    final_g = 1.0 + 0.1 * jax.random.normal(ks[12], (D_MODEL,), f32)
    return {"x": x, "c": c, "ada_w": ada_w, "ada_b": ada_b, "norm_g": norm_g,
            "ffn_w_in": ffn_w_in, "ffn_w_out": ffn_w_out,
            "pool_w": pool_w, "pool_scale": pool_scale,
            "conv_w_in": conv_w_in, "conv_w": conv_w, "conv_w_out": conv_w_out,
            "final_g": final_g}

def first_block(x, c, ada_w, ada_b, norm_g, ffn_w_in, ffn_w_out, pool_w, pool_scale,
              conv_w_in, conv_w, conv_w_out, final_g):
    B = x.shape[0]
    cond = jax.nn.silu(c)
    for i in range(DEPTH):
        mod = (cond @ ada_w[i] + ada_b[i]).reshape(B, N_SUB, N_MOD, D_MODEL)
        shift, scale, gate = mod[:, :, 0], mod[:, :, 1], mod[:, :, 2]

        h = modulate(rms_norm(x, norm_g[i, 0]), shift[:, 0], scale[:, 0])
        x = x + 0.5 * gate[:, 0, None, :] * swiglu(h, ffn_w_in[i, 0], ffn_w_out[i, 0])

        h = modulate(rms_norm(x, norm_g[i, 1]), shift[:, 1], scale[:, 1])
        j = i // N_MIXERS
        if i % N_MIXERS == 0:
            y = pool_mixer(h, pool_w[j], pool_scale[j])
        else:
            y = conv_mixer(h, conv_w_in[j], conv_w[j], conv_w_out[j])
        x = x + gate[:, 1, None, :] * y

        h = modulate(rms_norm(x, norm_g[i, 2]), shift[:, 2], scale[:, 2])
        x = x + 0.5 * gate[:, 2, None, :] * swiglu(h, ffn_w_in[i, 1], ffn_w_out[i, 1])
    return rms_norm(x, final_g)


DEPTH_2 = 1

D_MIX = D_MODEL
SB_HEADS = 8
SB_HEAD_DIM = 64
D_SB = SB_HEADS * SB_HEAD_DIM
D_RG = D_MIX - D_SB
RG_BLOCKS = 8
RG_BLOCK_DIM = D_RG // RG_BLOCKS
CONV_WIDTH_2 = 4
RG_C = 8.0
D_IN_PROJ = 3 * D_SB + 2 * D_RG
Q_BLOCK = 128
PEER_HEADS = 8
PEER_N_KEYS = 128
PEER_N_EXPERTS = PEER_N_KEYS * PEER_N_KEYS
PEER_D_KEY = 256
PEER_HALF = PEER_D_KEY // 2
PEER_TOPK = 16
TOKEN_CHUNK = 128
EPS = 1e-6


def rms_norm_2(x, g):
    xf = x.astype(jnp.float32)
    y = xf * lax.rsqrt(jnp.mean(xf * xf, axis=-1, keepdims=True) + EPS)
    return (y * g.astype(jnp.float32)).astype(x.dtype)

def stick_breaking_attention(q, k, v):
    B, H, S, Dh = q.shape
    nb = S // Q_BLOCK
    scale = Dh ** -0.5
    kpos = jnp.arange(S)

    def block(i):
        q_blk = lax.dynamic_slice_in_dim(q, i * Q_BLOCK, Q_BLOCK, axis=2)
        qpos = i * Q_BLOCK + jnp.arange(Q_BLOCK)
        causal = kpos[None, :] < qpos[:, None]
        z = jnp.einsum('bhqd,bhkd->bhqk', q_blk, k).astype(jnp.float32) * scale
        log_beta = jax.nn.log_sigmoid(z)
        log_one_minus = jnp.where(causal, jax.nn.log_sigmoid(-z), 0.0)
        suffix = lax.cumsum(log_one_minus, axis=3, reverse=True) - log_one_minus
        w = jnp.where(causal, jnp.exp(log_beta + suffix), 0.0)
        return jnp.einsum('bhqk,bhkd->bhqd', w.astype(v.dtype), v)

    out = lax.map(block, jnp.arange(nb))
    return out.transpose(1, 2, 0, 3, 4).reshape(B, H, S, Dh)

def causal_depthwise_conv(x, w, bias):
    S = x.shape[1]
    xp = jnp.pad(x, ((0, 0), (CONV_WIDTH_2 - 1, 0), (0, 0)))
    y = xp[:, 0:S, :] * w[0]
    for j in range(1, CONV_WIDTH_2):
        y = y + xp[:, j:j + S, :] * w[j]
    return y + bias

def rg_lru(x, w_a, b_a, w_x, b_x, lam):
    B, S, C = x.shape
    xb = x.reshape(B, S, RG_BLOCKS, RG_BLOCK_DIM)
    r = jax.nn.sigmoid(jnp.einsum('bsni,nij->bsnj', xb, w_a).reshape(B, S, C) + b_a)
    i_gate = jax.nn.sigmoid(jnp.einsum('bsni,nij->bsnj', xb, w_x).reshape(B, S, C) + b_x)
    log_a = -RG_C * r.astype(jnp.float32) * jax.nn.softplus(-lam.astype(jnp.float32))
    a = jnp.exp(log_a)
    b = jnp.sqrt(-jnp.expm1(2.0 * log_a)) * (i_gate * x).astype(jnp.float32)

    def step(h, ab):
        a_t, b_t = ab
        h = a_t * h + b_t
        return h, h

    h0 = jnp.zeros((B, C), jnp.float32)
    _, hs = lax.scan(step, h0, (a.transpose(1, 0, 2), b.transpose(1, 0, 2)))
    return hs.transpose(1, 0, 2).astype(x.dtype)

def peer_ffn(x, w_query, sub_keys, expert_u, expert_v):
    B, S, D = x.shape
    T = B * S
    xt = x.reshape(T // TOKEN_CHUNK, TOKEN_CHUNK, D)

    def chunk(xc):
        q = jnp.einsum('td,dhk->thk', xc, w_query)
        q = q.reshape(TOKEN_CHUNK, PEER_HEADS, 2, PEER_HALF)
        s = jnp.einsum('thpk,hpnk->thpn', q, sub_keys).astype(jnp.float32)
        top_s, top_i = lax.top_k(s, PEER_TOPK)
        cand_s = top_s[:, :, 0, :, None] + top_s[:, :, 1, None, :]
        cand_i = top_i[:, :, 0, :, None] * PEER_N_KEYS + top_i[:, :, 1, None, :]
        cand_s = cand_s.reshape(TOKEN_CHUNK, PEER_HEADS, PEER_TOPK * PEER_TOPK)
        cand_i = cand_i.reshape(TOKEN_CHUNK, PEER_HEADS, PEER_TOPK * PEER_TOPK)
        best_s, best_pos = lax.top_k(cand_s, PEER_TOPK)
        idx = jnp.take_along_axis(cand_i, best_pos, axis=-1)
        g = jax.nn.softmax(best_s, axis=-1)
        u = jnp.take(expert_u, idx, axis=0)
        v = jnp.take(expert_v, idx, axis=0)
        act = jax.nn.gelu(jnp.einsum('td,thkd->thk', xc, u))
        return jnp.einsum('thk,thkd->td', (g * act).astype(v.dtype), v)

    y = lax.map(chunk, xt)
    return y.reshape(B, S, D)

def second_inputs(seed: int = 0) -> dict:
    key = jax.random.key(seed)
    ks = jax.random.split(key, 24)
    f32 = jnp.float32

    def nrm(k, shape, scale):
        return jax.random.normal(k, shape, f32) * scale

    def gain(k, shape):
        return 1.0 + 0.02 * jax.random.normal(k, shape, f32)

    u_a = jax.random.uniform(ks[11], (DEPTH_2, D_RG), f32, 0.9, 0.999)
    a_base = u_a ** (1.0 / RG_C)
    rg_lambda = jnp.log(a_base) - jnp.log1p(-a_base)
    return {
        "x": jax.random.normal(ks[0], (BATCH, SEQ, D_MODEL), f32),
        "norm_mix": gain(ks[1], (DEPTH_2, D_MODEL)),
        "w_in": nrm(ks[2], (DEPTH_2, D_MODEL, D_IN_PROJ), D_MODEL ** -0.5),
        "q_norm": gain(ks[3], (DEPTH_2, SB_HEAD_DIM)),
        "k_norm": gain(ks[4], (DEPTH_2, SB_HEAD_DIM)),
        "conv_w": nrm(ks[5], (DEPTH_2, CONV_WIDTH_2, D_RG), CONV_WIDTH_2 ** -0.5),
        "conv_b": nrm(ks[6], (DEPTH_2, D_RG), 0.01),
        "rg_w_a": nrm(ks[7], (DEPTH_2, RG_BLOCKS, RG_BLOCK_DIM, RG_BLOCK_DIM), RG_BLOCK_DIM ** -0.5),
        "rg_b_a": nrm(ks[8], (DEPTH_2, D_RG), 0.01),
        "rg_w_x": nrm(ks[9], (DEPTH_2, RG_BLOCKS, RG_BLOCK_DIM, RG_BLOCK_DIM), RG_BLOCK_DIM ** -0.5),
        "rg_b_x": nrm(ks[10], (DEPTH_2, D_RG), 0.01),
        "rg_lambda": rg_lambda,
        "out_norm_sb": gain(ks[12], (DEPTH_2, D_SB)),
        "out_norm_rg": gain(ks[13], (DEPTH_2, D_RG)),
        "w_out": nrm(ks[14], (DEPTH_2, D_MIX, D_MODEL), D_MIX ** -0.5),
        "norm_ffn": gain(ks[15], (DEPTH_2, D_MODEL)),
        "peer_w_query": nrm(ks[16], (DEPTH_2, D_MODEL, PEER_HEADS, PEER_D_KEY), D_MODEL ** -0.5),
        "peer_sub_keys": nrm(ks[17], (DEPTH_2, PEER_HEADS, 2, PEER_N_KEYS, PEER_HALF), PEER_HALF ** -0.5),
        "peer_u": nrm(ks[18], (DEPTH_2, PEER_N_EXPERTS, D_MODEL), D_MODEL ** -0.5),
        "peer_v": nrm(ks[19], (DEPTH_2, PEER_N_EXPERTS, D_MODEL), PEER_HEADS ** -0.5),
    }

def second_block(x, norm_mix, w_in, q_norm, k_norm, conv_w, conv_b, rg_w_a, rg_b_a,
              rg_w_x, rg_b_x, rg_lambda, out_norm_sb, out_norm_rg, w_out, norm_ffn,
              peer_w_query, peer_sub_keys, peer_u, peer_v):
    B, S, _ = x.shape
    for l in range(DEPTH_2):
        h = rms_norm_2(x, norm_mix[l])
        proj = jnp.einsum('bsd,de->bse', h, w_in[l])
        q = proj[:, :, 0:D_SB]
        k = proj[:, :, D_SB:2 * D_SB]
        v = proj[:, :, 2 * D_SB:3 * D_SB]
        x_rg = proj[:, :, 3 * D_SB:3 * D_SB + D_RG]
        g_rg = proj[:, :, 3 * D_SB + D_RG:D_IN_PROJ]

        def to_heads(t):
            return t.reshape(B, S, SB_HEADS, SB_HEAD_DIM).transpose(0, 2, 1, 3)

        qh = rms_norm_2(to_heads(q), q_norm[l])
        kh = rms_norm_2(to_heads(k), k_norm[l])
        o_sb = stick_breaking_attention(qh, kh, to_heads(v))
        o_sb = o_sb.transpose(0, 2, 1, 3).reshape(B, S, D_SB)

        x_rg = causal_depthwise_conv(x_rg, conv_w[l], conv_b[l])
        o_rg = rg_lru(x_rg, rg_w_a[l], rg_b_a[l], rg_w_x[l], rg_b_x[l], rg_lambda[l])
        o_rg = o_rg * jax.nn.gelu(g_rg)

        mixed = jnp.concatenate(
            [rms_norm_2(o_sb, out_norm_sb[l]), rms_norm_2(o_rg, out_norm_rg[l])], axis=-1)
        x = x + jnp.einsum('bse,ed->bsd', mixed, w_out[l])

        h = rms_norm_2(x, norm_ffn[l])
        x = x + peer_ffn(h, peer_w_query[l], peer_sub_keys[l], peer_u[l], peer_v[l])
    return x


def setup_inputs(seed=0):
    out = dict(first_inputs(seed))
    for name, value in second_inputs(seed + 1).items():
        if name != "x":
            out[name + "_2"] = value
    return out


def reference(
    x, c, ada_w, ada_b, norm_g, ffn_w_in, ffn_w_out, pool_w, pool_scale, conv_w_in, conv_w,
    conv_w_out, final_g, norm_mix_2, w_in_2, q_norm_2, k_norm_2, conv_w_2, conv_b_2, rg_w_a_2,
    rg_b_a_2, rg_w_x_2, rg_b_x_2, rg_lambda_2, out_norm_sb_2, out_norm_rg_2, w_out_2,
    norm_ffn_2, peer_w_query_2, peer_sub_keys_2, peer_u_2, peer_v_2,
):
    x = first_block(
        x, c, ada_w, ada_b, norm_g, ffn_w_in, ffn_w_out, pool_w, pool_scale, conv_w_in, conv_w,
        conv_w_out, final_g,
    )
    return second_block(
        x, norm_mix_2, w_in_2, q_norm_2, k_norm_2, conv_w_2, conv_b_2, rg_w_a_2, rg_b_a_2,
        rg_w_x_2, rg_b_x_2, rg_lambda_2, out_norm_sb_2, out_norm_rg_2, w_out_2, norm_ffn_2,
        peer_w_query_2, peer_sub_keys_2, peer_u_2, peer_v_2,
    )


_drawn_inputs = setup_inputs


def setup_inputs(seed=0):
    import zlib

    import numpy as np

    out = dict(_drawn_inputs(seed))
    spreads = {}
    factors = {'q_norm_2': 5.19,
     'k_norm_2': 5.398,
     'rg_b_a_2': 32.041,
     'rg_b_x_2': 8.0,
     'out_norm_sb_2': 9.241,
     'out_norm_rg_2': 9.088,
     'norm_ffn_2': 9.897}
    for name, (base, spread) in spreads.items():
        noise = np.random.default_rng([zlib.crc32(name.encode()), seed]).standard_normal(out[name].shape)
        drawn = base * np.exp(spread * noise) if base else spread * noise
        out[name] = __import__('jax').numpy.asarray(drawn.astype(out[name].dtype))
    for name, factor in factors.items():
        out[name] = (out[name] * factor).astype(out[name].dtype)
    return out
```

```python
import concourse.bass as bass
from concourse import mybir
import numpy as np

F32 = mybir.dt.float32
F32R = mybir.dt.float32r
BF16 = mybir.dt.bfloat16
U32 = mybir.dt.uint32
ALU = mybir.AluOpType
ACT = mybir.ActivationFunctionType
AXX = mybir.AxisListType.X

P = 128
T = 512
D = 1024
KT = D // P
FF = 2816
FT = FF // P
GB = 8
R = 4
LOOK = 3

SEG = {}
_at = 0
for _name, _n in (("ffn0_in", 2 * FT), ("ffn0_out", FT), ("pool", 2),
                  ("ffn1_in", 2 * FT), ("ffn1_out", FT),
                  ("ffn2_in", 2 * FT), ("ffn2_out", FT),
                  ("conv_in", 24), ("conv_out", 8),
                  ("ffn3_in", 2 * FT), ("ffn3_out", FT),
                  ("xr", 4), ("qk", 8), ("gates", 1), ("gr", 4), ("v", 4), ("mix_out", 8),
                  ("query", 16), ("up", 128), ("down", 128)):
    SEG[_name] = (_at, _n)
    _at += _n
NORM_TILES = (8, 8, 8, 8, 8, 8, 8, 8, 4, 4, 8)
ALL_NORMS = tuple(range(11))
SPLIT_NORMS = (0, 2, 3, 4, 5, 7, 8, 9, 10)
SCALED_NORMS = (0, 1) + SPLIT_NORMS[1:]
DECAY_STEPS = 18
CORR = {2: 0, 4: 1, 8: 4, 16: 11}
N_GROUPS = _at

SMALL = {}
_at = 0
for _name, _n in (("c", KT), ("ada_b", 18 * KT), ("norm_g", 6 * KT), ("pool_scale", KT),
                  ("conv_w", 3 * KT), ("final_g", KT), ("zero", KT), ("eps", 1)):
    SMALL[_name] = _at
    _at += _n
N_SMALL = _at

SMALL2 = {}
_at = 0
for _name, _n in (("norm_mix", KT), ("q_gain", 1), ("k_gain", 1), ("conv_w2", 16), ("conv_b2", 4),
                  ("b_a", 4), ("b_x", 4), ("lam", 4), ("out_gain", KT), ("norm_ffn", KT),
                  ("zero2", KT), ("eps2", 1)):
    SMALL2[_name] = _at
    _at += _n
N_SMALL2 = _at

HEADS = 8
CT = 4
N_PLAIN = 5
BLK, MASK, MEAN_H, IDENT, IOTA = range(N_PLAIN)
TRI, ONES, IDENT_R, FAR = range(4)
ATT_OFF = [0, 512, 896, 1152]
ATT_COLS = 1280
PH = 8
HP = 2 * PH
NK = 128
TOP = 16
TT = T // P
TC = 8
MB = 8
NB = NK // MB
LEAD = 8
CHUNKS = P // TC
GAP = 8
assert TT * (LEAD + CHUNKS + GAP) == NK and LEAD % 4 == GAP % 4 == CHUNKS % 4 == 0
LOWEST = -3.0e38
UNITS = [(h, i) for h in range(HEADS) for i in reversed(range(CT))]


def at(c, i, m):
    return c if i is None else i * m + c


def tiles_before(norms, n):
    return sum(NORM_TILES[m] for m in norms if m < n)


def v_group(b, d):
    return SEG["down"][0] + MB * b + d


def build(nc, stream, ada, smalls, consts, smalls2, consts2, keys, xin, out):
    KB = 1024

    def place(name, kib, shape, dt):
        return nc.alloc_sbuf_tensor_at(name, shape, dt, offset=base + int(kib * KB))

    base = (nc.sbuf_base + 63) // 64 * 64
    raw = place("raw", 0, [P, R, GB, P], F32)
    whi = place("whi", 16, [P, R, GB, P], F32R)
    wlo = place("wlo", 32, [P, R, GB, P], F32R)
    x = place("x", 48, [P, KT, T], F32)
    hhi = place("hhi", 64, [P, KT, T], F32R)
    hlo = place("hlo", 80, [P, KT, T], F32R)
    small = place("small", 96, [P, N_SMALL], F32)
    mod = place("mod", 97.25, [P, 18 * KT], F32)
    coef = place("coef", 97.875, [P, 2, 6 * KT], F32)
    cond = place("cond", 98.5, [P, KT], F32)
    one_col = place("one_col", 98.625, [P, 1], F32)
    corr = place("corr", 98.75, [P, 32], F32)
    mean_d = place("mean_d", 99, [P, P], F32)
    uhi = place("uhi", 99.5, [P, FT, T], F32R)
    ulo = place("ulo", 143.5, [P, FT, T], F32R)
    silu = place("silu", 187.5, [P, 2, T], F32)
    u32 = place("u32", 191.5, [P, 2, T], F32)
    ada_raw = place("ada_raw", 195.5, [P, 4, T], F32)
    ada_accs = [place(f"ada_acc{h}", 203.5 + 2 * h, [P, T], F32) for h in range(2)]
    sq = place("sq", 102, [P, 2, T], F32)
    sqsum = place("sqsum", 106, [P, T], F32)
    std = place("std", 108, [P, T], F32)
    rstd = place("rstd", 110, [P, T], F32)
    xn = place("xn", 112, [P, 2, T], F32)
    h32 = place("h32", 116, [P, 2, T], F32)
    pad0 = place("pad0", 120, [P, 2, 16 + T], F32)
    pad1 = place("pad1", 125, [P, 16 + T], F32)
    pad2 = place("pad2", 128, [P, 16 + T], F32)
    mix32 = place("mix32", 131, [P, 2, T], F32)
    yhi = place("yhi", 136, [P, KT, T], F32R)
    ylo = place("ylo", 152, [P, KT, T], F32R)
    cgate = place("cgate", 168, [P, 2, T], F32)
    cu = place("cu", 172, [P, 2, 2 + T], F32)
    cv = place("cv", 177, [P, 2, T], F32)
    y32 = place("y32", 181, [P, 2, T], F32)

    q_hi = place("q_hi", 100, [P, CT, T], F32R)
    q_lo = place("q_lo", 108, [P, CT, T], F32R)
    k_hi = place("k_hi", 116, [P, CT, T], F32R)
    k_lo = place("k_lo", 124, [P, CT, T], F32R)
    v_hi = place("v_hi", 132, [P, CT, T], F32R)
    v_lo = place("v_lo", 140, [P, CT, T], F32R)
    o = place("o", 148, [P, KT, T], F32)
    xpad = place("xpad", 164, [P, 2, 8 + T], F32)
    qsq = place("qsq", 168.25, [P, 2, T], F32)
    xc = place("xc", 172.25, [P, CT, T], F32)
    xc_hi = place("xc_hi", 148, [P, CT, T], F32R)
    xc_lo = place("xc_lo", 156, [P, CT, T], F32R)
    qstd = place("qstd", 184.25, [P, T], F32)
    qrstd = place("qrstd", 186.25, [P, T], F32)
    r_gate = place("r_gate", 188.25, [P, CT, T], F32)
    i_gate = place("i_gate", 140, [P, CT, T], F32)
    a_dec = place("a_dec", 148, [P, CT, T], F32)
    tanh_a = place("tanh_a", 156, [P, CT, T], F32)
    qn = place("qn", 132, [P, 2, T], F32)
    cx = place("cx", 136, [P, 2, T], F32)
    sp = place("sp", 164, [P, 2, T], F32)
    l_hi = place("l_hi", 168, [P, 2, ATT_COLS], F32R)
    l_lo = place("l_lo", 178, [P, 2, ATT_COLS], F32R)
    w32 = place("w32", 188, [P, 2, T], F32)
    w_hi = place("w_hi", 192, [P, 2, T], F32R)
    w_lo = place("w_lo", 196, [P, 2, T], F32R)
    small2 = place("small2", 202.5, [P, N_SMALL2], F32)
    decay = place("decay", 203, [P, 8, CT], F32)
    sq_plain = place("sq_plain", 203.25, [P, N_PLAIN, P], F32)
    sq_round = place("sq_round", 205.75, [P, 4, P], F32R)

    key_hi = place("key_hi", 122, [P, HP, NK], F32R)
    key_lo = place("key_lo", 130, [P, HP, NK], F32R)
    key32 = place("key32", 138, [P, HP, NK], F32)
    qt_hi = place("qt_hi", 146, [P, 2, T], F32R)
    qt_lo = place("qt_lo", 150, [P, 2, T], F32R)
    top_v = place("top_v", 154, [P, PH, 2, TT, TOP], F32)
    top_i = place("top_i", 158, [P, PH, 2, TT, TOP], U32)
    top_b = place("top_b", 162, [P, PH, 2, TT, TOP], BF16)
    rest1 = place("rest1", 178, [P, TT, NK], F32)
    cand = place("cand", 122, [P, PH, TOP * TOP], F32)
    rest2 = place("rest2", 130, [P, PH, TOP * TOP], F32)
    is_pos = place("is_pos", 138, [P, PH, TOP, TOP], BF16)
    prod = place("prod", 142, [P, PH, TOP, TOP], BF16)
    best_v = place("best_v", 190, [P, PH, TOP], F32)
    best_p = place("best_p", 190.5, [P, PH, TOP], U32)
    pos_u = place("pos_u", 191, [P, 2, PH, TOP], U32)
    pos_b = place("pos_b", 192, [P, 2, PH, TOP], BF16)
    below = place("below", 192.5, [P, PH, TOP], F32)
    expo = place("expo", 193, [P, PH, TOP], F32)
    esum = place("esum", 193.5, [P, 2, PH], F32)
    chosen = place("chosen", 194, [P, 3, PH * TOP], F32)
    left = place("left", 195.5, [P, 2, P], F32)
    iota_b = place("iota_b", 202, [P, P], BF16)
    hot_n = place("hot_n", 177, [P, 2, TC, P], BF16)
    hot_m = place("hot_m", 181, [P, 2, TC, P], BF16)
    hot_w = place("hot_w", 185, [P, 2, 3, TC, P], BF16)
    pick = place("pick", 197, [P, 5, T], BF16)
    spread = place("spread", 100, [P, NK, P], F32)
    g_ring = place("g_ring", 100, [P, 4, T], F32)
    act_out = place("act_out", 164, [P, 4, T], F32)
    act_in = place("act_in", 108, [P, 4, T], F32)
    we32 = place("we32", 180, [P, 2, T], F32)
    we_hi = place("we_hi", 116, [P, 2 * MB, T], F32R)
    we_lo = place("we_lo", 148, [P, 2 * MB, T], F32R)

    expert_weights = nc.dram_tensor("expert_weights", (TT, P, NK, P), F32).ap()
    expert_acts = nc.dram_tensor("expert_acts", (NK, P, T), F32).ap()

    psum = [nc.alloc_psum_tensor(f"bank{b}", [P, T], F32) for b in range(8)]

    sems = {}

    def sem(name):
        if name not in sems:
            sems[name] = nc.alloc_semaphore(name)
        return sems[name]

    const_landed = sem("const_landed")
    raw_landed = [sem(f"raw_landed{s}") for s in range(R)]
    hi_ready = sem("hi_ready")
    lo_ready = sem("lo_ready")
    pe_groups = sem("pe_groups")
    x_ready = sem("x_ready")
    sq_ready = sem("sq_ready")
    sq_used = sem("sq_used")
    ms_ready = sem("ms_ready")
    std_ready = sem("std_ready")
    rstd_ready = sem("rstd_ready")
    xn_ready = sem("xn_ready")
    h32_ready = sem("h32_ready")
    hhi_ready = sem("hhi_ready")
    h_ready = sem("h_ready")
    silu_ready = sem("silu_ready")
    u_mul = sem("u_mul")
    uhi_ready = sem("uhi_ready")
    u_ready = sem("u_ready")
    cond_ready = sem("cond_ready")
    setup_done = sem("setup_done")
    ada_landed = [sem(f"ada_landed{s}") for s in range(4)]
    ada_used = sem("ada_used")
    ada_summed = sem("ada_summed")
    mod_ready = sem("mod_ready")
    coef_ready = sem("coef_ready")
    pool_h = sem("pool_h")
    pool_step = sem("pool_step")
    pool_mixed = sem("pool_mixed")
    pool_hi = sem("pool_hi")
    pool_ready = sem("pool_ready")
    cgate_ready = sem("cgate_ready")
    cu_ready = sem("cu_ready")
    cv_step = sem("cv_step")
    y32_ready = sem("y32_ready")
    yhi_ready = sem("yhi_ready")
    y_ready = sem("y_ready")
    out_done = sem("out_done")
    const2_landed = sem("const2_landed")
    const2_ready = sem("const2_ready")
    decay_step = sem("decay_step")
    decay_exp = sem("decay_exp")
    xpad_ready = sem("xpad_ready")
    conv2_step = sem("conv2_step")
    xc_ready = sem("xc_ready")
    xc_hi_ready = sem("xc_hi_ready")
    xc_lo_ready = sem("xc_lo_ready")
    qsq_ready = sem("qsq_ready")
    qms_ready = sem("qms_ready")
    qstd_ready = sem("qstd_ready")
    qrstd_ready = sem("qrstd_ready")
    qn_ready = sem("qn_ready")
    qhi_ready = sem("qhi_ready")
    q_ready = sem("q_ready")
    gate_products = sem("gate_products")
    gates_ready = sem("gates_ready")
    tanh_ready = sem("tanh_ready")
    a_ready = sem("a_ready")
    rg_step = sem("rg_step")
    rg_neg = sem("rg_neg")
    rg_root = sem("rg_root")
    gelu_ready = sem("gelu_ready")
    rg_done = sem("rg_done")
    vhi_ready = sem("vhi_ready")
    v_ready = sem("v_ready")
    z_ready = sem("z_ready")
    lnx_step = sem("lnx_step")
    sp_ready = sem("sp_ready")
    lhi_ready = sem("lhi_ready")
    l_ready = sem("l_ready")
    expo_ready = sem("expo_ready")
    w32_ready = sem("w32_ready")
    whi_ready = sem("whi_ready")
    w_ready = sem("w_ready")
    pv_done = sem("pv_done")
    o_ready = sem("o_ready")
    rg_out = sem("rg_out")
    keys_landed = sem("keys_landed")
    keys_hi = sem("keys_hi")
    keys_ready = sem("keys_ready")
    qthi_ready = sem("qthi_ready")
    qt_ready = sem("qt_ready")
    scores_done = sem("scores_done")
    top_step = sem("top_step")
    sel_step = sem("sel_step")
    below_ready = sem("below_ready")
    exp_ready = sem("exp_ready")
    chosen_ready = sem("chosen_ready")
    turned = sem("turned")
    pick_step = sem("pick_step")
    iota_ready = sem("iota_ready")
    hot_mark = sem("hot_mark")
    hot_ready = sem("hot_ready")
    hot_third = sem("hot_third")
    hot_used = sem("hot_used")
    spread_ready = sem("spread_ready")
    spilled = sem("spilled")
    acts_stored = [sem(f"acts_stored{s}") for s in range(4)]
    a_landed = [sem(f"a_landed{s}") for s in range(4)]
    g_landed = [sem(f"g_landed{s}") for s in range(4)]
    gelu_done = sem("gelu_done")
    we_mul = sem("we_mul")
    we_hi_ready = sem("we_hi_ready")
    we_ready = sem("we_ready")
    y_added = sem("y_added")

    def S(name, k=0, n=1):
        return small[:, SMALL[name] + k:SMALL[name] + k + n]

    def S2(name, k=0, n=1):
        return small2[:, SMALL2[name] + k:SMALL2[name] + k + n]

    def hot_column(part, c, i):
        cols = pick[:, part, TC * c:TC * c + TC] if i is None else pick[:, part, bass.ds(i * (4 * TC) + TC * c, TC)]
        return cols.unsqueeze(2).to_broadcast([P, TC, P])

    ADA_NEW = {0: 6, 1: 9, 2: 0, 3: 0}
    ADA_AT = {0: 3, 1: 9}
    SUB_NORM = {0: 0, 1: 2, 2: 3, 3: 5}
    n_groups = N_GROUPS

    with nc.Block() as block:

        @block.sync
        def _(sp):
            sp.dma_start(small[:, :], smalls).then_inc(const_landed, 16)
            sp.dma_start(mean_d[:, :], consts[:, 0:P]).then_inc(const_landed, 16)
            sp.dma_start(corr[:, :], consts[:, P:P + 32]).then_inc(const_landed, 16)
            sp.dma_start(x[:, :, :], xin).then_inc(const_landed, 16)

            def load(c, i, m):
                s = c % R
                if c >= R:
                    sp.wait_ge(lo_ready, at(c - R + 1, i, m))
                sp.dma_start(raw[:, s, :, :], stream[at(c, i, m)] if i is None else stream[bass.ds(i * m + c, 1)].rearrange("a p g n -> (a p) g n")).then_inc(raw_landed[s], 16)

            for c in range(R):
                load(c, None, 0)
            n = (n_groups - R) // R
            with sp.Fori(0, n) as i:
                for j in range(R):
                    load(R + j, i, R)
            for c in range(R + n * R, n_groups):
                load(c, None, 0)
            sp.wait_ge(y_added, NB * KT)
            sp.dma_start(out, x[:, :, :]).then_inc(out_done, 16)
            sp.wait_ge(out_done, 16)

        @block.gpsimd
        def _(pool):
            def lo(c, i, m):
                s = c % R
                pool.wait_ge(hi_ready, at(c + 1, i, m))
                pool.tensor_tensor(wlo[:, s, :, :], raw[:, s, :, :], whi[:, s, :, :].bitcast(F32),
                                   ALU.subtract).then_inc(lo_ready, 1)

            def lo_range(first, last):
                n = (last - first) // R
                with pool.Fori(0, n) as i:
                    for j in range(first, first + R):
                        lo(j, i, R)
                for c in range(first + n * R, last):
                    lo(c, None, 0)

            up = SEG["up"][0]
            lo_range(0, up + LOOK)

            def third_rows(c, i):
                pool.wait_ge(hot_mark, at(c + 1, i, 4))
                if c >= 2:
                    pool.wait_ge(hot_used, at(c - 1, i, 4))
                pool.tensor_tensor(hot_w[:, c % 2, 2, :, :], hot_m[:, c % 2, :, :], hot_column(4, c, i), ALU.mult).then_inc(hot_third, 1)

            def columns_run(m0, n):
                with pool.Fori(0, n // 4) as i:
                    for m in range(m0, m0 + 4):
                        lo(up + m + LOOK, i, 4)

            columns_run(0, TT * LEAD)
            for tt in range(TT):
                m0 = TT * LEAD + tt * (CHUNKS + GAP)
                c0 = tt * CHUNKS
                if tt == 0:
                    for k in range(4):
                        lo(up + m0 + k + LOOK, None, 0)
                        third_rows(c0 + k, None)
                    m0, c0 = m0 + 4, c0 + 4
                with pool.Fori(0, CHUNKS // 4 - (tt == 0)) as i:
                    for k in range(4):
                        lo(up + m0 + k + LOOK, i, 4)
                        third_rows(c0 + k, i)
                columns_run(TT * LEAD + tt * (CHUNKS + GAP) + CHUNKS, GAP)
            lo_range(up + NK + LOOK, n_groups)

        @block.scalar
        def _(act):
            def hi(c, i=None, m=0):
                if c >= n_groups:
                    return
                s = c % R
                act.wait_ge(raw_landed[s], at(16 * (c // R + 1), i, 16 * m // R))
                if c >= R:
                    act.wait_ge(pe_groups, at(c - R + 1, i, m))
                act.activation(whi[:, s, :, :], raw[:, s, :, :], ACT.Copy).then_inc(hi_ready, 1)

            def ada_load(c, i=None, m=0):
                s = c % 4
                if c >= 4:
                    act.wait_ge(ada_used, at(c - 3, i, m))
                it, hf, k = c // 16, c // 8 % 2, c % 8
                if i is None:
                    src = ada[(it // 9) * KT + k, :, ((it % 9) * 2 + hf) * T:((it % 9) * 2 + hf + 1) * T]
                else:
                    src = ada[(it // 9) * KT + k, :, bass.ds(i * (2 * T) + ((it % 9) * 2 + hf) * T, T)]
                act.dma_start(ada_raw[:, s, :], src).then_inc(ada_landed[s], 16)

            def norm(n, scale, shift, h_out, src=x, t0=0):
                s0 = tiles_before(ALL_NORMS, n)
                for k in range(NORM_TILES[n]):
                    if n == 0 and k == 0:
                        act.wait_ge(const_landed, 64)
                    elif 0 < n < 8 or n == 10:
                        act.wait_ge(x_ready, KT * (min(n, 8) - 1) + k + 1)
                    if s0 + k >= 2:
                        act.wait_ge(sq_used, s0 + k - 1)
                    act.activation(sq[:, k % 2, :], src[:, t0 + k, :], ACT.Square).then_inc(sq_ready, 1)
                act.wait_ge(ms_ready, n + 1)
                act.activation(std[:, :], psum[7][:, :], ACT.Sqrt, bias=eps(n)).then_inc(std_ready, 1)
                if scale is None:
                    return
                if n < 6:
                    act.wait_ge(coef_ready, 2 * (n + 1))
                for k in range(NORM_TILES[n]):
                    act.wait_ge(xn_ready, tiles_before(SCALED_NORMS, n) + k + 1)
                    h_out(n, k, scale[:, k:k + 1], shift[:, k:k + 1])

            def eps(n):
                return S("eps") if n < 7 else S2("eps2")

            def h_split(n, k, sc, sh):
                if k >= 2:
                    act.wait_ge(h_ready, tiles_before(SPLIT_NORMS, n) + k - 1)
                act.activation(h32[:, k % 2, :], xn[:, k % 2, :], ACT.Identity, bias=sh, scale=sc).then_inc(h32_ready, 1)
                act.activation(hhi[:, k + (4 if n == 9 else 0), :], xn[:, k % 2, :], ACT.Identity, bias=sh, scale=sc).then_inc(hhi_ready, 1)

            def sublayer(n):
                return coef[:, 0, n * KT:(n + 1) * KT], mod[:, 3 * n * KT:(3 * n + 1) * KT]

            def ffn(q):
                g0 = SEG[f"ffn{q}_in"][0]
                new = ADA_NEW[q]
                u0 = 16 * ADA_AT.get(q, 0)

                def tile(j, i, units):
                    g = g0 + 2 * j
                    t = FT * q + j
                    hi(g + LOOK, i, 4)
                    hi(g + LOOK + 1, i, 4)
                    act.wait_ge(pe_groups, at(g + 1, i, 4))
                    if t >= 2:
                        act.wait_ge(u_mul, at(t - 1, i, 2))
                    act.activation(silu[:, j % 2, :], psum[2 * (j % 2)][:, :], ACT.Silu).then_inc(silu_ready, 1)
                    act.wait_ge(u_mul, at(t + 1, i, 2))
                    act.activation(uhi[:, at(j, i, 2), :] if i is None else uhi[:, bass.ds(i * 2 + j, 1), :].rearrange("p a t -> p (a t)"), u32[:, j % 2, :], ACT.Copy).then_inc(uhi_ready, 1)
                    if units:
                        for k in range(8):
                            ada_load(u0 + 8 * (j % 2) + k + 16 * (j // 2), i, 16)

                for j in range(2):
                    tile(j, None, new > 0)
                if new > 1:
                    with act.Fori(0, new - 1) as i:
                        for j in range(2, 4):
                            tile(j, i, True)
                rest = FT // 2 - max(new, 1)
                with act.Fori(0, rest) as i:
                    for j in range(2 * max(new, 1), 2 * max(new, 1) + 2):
                        tile(j, i, False)
                g1 = SEG[f"ffn{q}_out"][0]
                for half in range(2):
                    c = g1 + half * (FT // 2) + LOOK
                    hi(c)
                    with act.Fori(0, 2) as i:
                        for j in range(4):
                            hi(c + 1 + j, i, 4)
                    hi(c + 9)
                    hi(c + 10)

            act.wait_ge(const_landed, 64)
            act.activation(cond[:, :], S("c", 0, KT), ACT.Silu).then_inc(cond_ready, 1)
            for u in range(48):
                ada_load(u)
            for c in range(LOOK):
                hi(c)
            norm(0, *sublayer(0), h_split)
            ffn(0)
            def pool_out(n, k, sc, sh):
                if k >= 2:
                    act.wait_ge(pool_mixed, k - 1)
                act.activation(pad0[:, k % 2, 16:16 + T], xn[:, k % 2, :], ACT.Identity, bias=sh, scale=sc).then_inc(pool_h, 1)
                if k >= 1:
                    pool_round(k - 1)

            def pool_round(k):
                act.wait_ge(pool_mixed, k + 1)
                act.activation(hhi[:, k, :], mix32[:, k % 2, :], ACT.Copy).then_inc(pool_hi, 1)

            act.wait_ge(setup_done, 2)
            norm(1, *sublayer(1), pool_out)
            pool_round(KT - 1)
            hi(SEG["pool"][0] + LOOK)
            hi(SEG["pool"][0] + LOOK + 1)
            norm(2, *sublayer(2), h_split)
            ffn(1)
            norm(3, *sublayer(3), h_split)
            ffn(2)
            norm(4, *sublayer(4), h_split)
            g0 = SEG["conv_in"][0]

            def conv_tile(j, i):
                g = g0 + 3 * j
                hi(g + LOOK, i, 12)
                act.wait_ge(pe_groups, at(g + 1, i, 12))
                if j >= 2:
                    act.wait_ge(cu_ready, at(j - 1, i, 4))
                act.activation(cgate[:, j % 2, :], psum[3 * (j % 2)][:, :], ACT.Copy).then_inc(cgate_ready, 1)
                hi(g + LOOK + 1, i, 12)
                hi(g + LOOK + 2, i, 12)
                act.wait_ge(y32_ready, at(j + 1, i, 4))
                act.activation(yhi[:, j, :], y32[:, j % 2, :], ACT.Copy).then_inc(yhi_ready, 1)

            for j in range(KT):
                conv_tile(j, None)
            g0 = SEG["conv_out"][0]
            for c in range(KT):
                hi(g0 + c + LOOK)
            norm(5, *sublayer(5), h_split)
            ffn(3)
            norm(6, None, None, None)
            act.dma_start(small2[:, :], smalls2).then_inc(const2_landed, 16)
            act.dma_start(sq_plain[:, :, :], consts2[:, 0:N_PLAIN, :]).then_inc(const2_landed, 16)
            act.dma_start(xc[:, 0, :], consts2[:, N_PLAIN:, :].rearrange("p a n -> p (a n)")).then_inc(const2_landed, 16)
            act.wait_ge(const2_landed, 48)
            act.activation(sq_round[:, :, :].rearrange("p a n -> p (a n)"), xc[:, 0, :], ACT.Copy).then_inc(const2_ready, 1)
            act.wait_ge(decay_step, 1)
            act.activation(decay[:, 1, :], decay[:, 0, :], ACT.Exp, scale=-1.0).then_inc(decay_exp, 1)
            norm(7, S2("norm_mix", 0, KT), S2("zero2", 0, KT), h_split)
            g0 = SEG["xr"][0]

            def round_xc(c):
                act.wait_ge(xc_ready, c + 1)
                act.activation(xc_hi[:, c, :], xc[:, c, :], ACT.Copy).then_inc(xc_hi_ready, 1)

            act.wait_ge(setup_done, 3)
            for c in range(CT):
                hi(g0 + c + LOOK)
                act.wait_ge(pe_groups, g0 + c + 1)
                if c >= 2:
                    act.wait_ge(xc_ready, c - 1)
                act.activation(xpad[:, c % 2, 8:8 + T], psum[c][:, :], ACT.Copy).then_inc(xpad_ready, 1)
                if c:
                    round_xc(c - 1)
            g0 = SEG["qk"][0]

            def q_std(t):
                act.wait_ge(qms_ready, t + 1)
                if t:
                    act.wait_ge(qrstd_ready, t)
                act.activation(qstd[:, :], psum[6 + t % 2][:, :], ACT.Sqrt, bias=S2("eps2")).then_inc(qstd_ready, 1)

            def q_round(t):
                act.wait_ge(qn_ready, t + 1)
                dst = q_hi if t < CT else k_hi
                act.activation(dst[:, t % CT, :], qn[:, t % 2, :], ACT.Copy).then_inc(qhi_ready, 1)

            for t in range(2 * CT):
                hi(g0 + t + LOOK)
                act.wait_ge(pe_groups, g0 + t + 1)
                if t >= 2:
                    act.wait_ge(qms_ready, t - 1)
                act.activation(qsq[:, t % 2, :], psum[4 + t % 2][:, :], ACT.Square).then_inc(qsq_ready, 1)
                if t == 0:
                    round_xc(CT - 1)
                if t:
                    q_std(t - 1)
                if t >= 2:
                    q_round(t - 2)
            q_std(2 * CT - 1)
            q_round(2 * CT - 2)
            q_round(2 * CT - 1)
            hi(SEG["gates"][0] + LOOK)
            act.wait_ge(decay_step, DECAY_STEPS)
            for c in range(CT):
                if c < CT - 1:
                    act.wait_ge(gate_products, c + 1)
                else:
                    act.wait_ge(pe_groups, SEG["gates"][0] + 1)
                b = 2 * (c % 2)
                act.activation(r_gate[:, c, :], psum[b][:, :], ACT.Sigmoid, bias=S2("b_a", c)).then_inc(gates_ready, 1)
                act.activation(i_gate[:, c, :], psum[b + 1][:, :], ACT.Sigmoid, bias=S2("b_x", c)).then_inc(gates_ready, 1)
                act.wait_ge(gates_ready, 2 * c + 2)
                act.activation(tanh_a[:, c, :], r_gate[:, c, :], ACT.Tanh, scale=decay[:, 7, c:c + 1]).then_inc(tanh_ready, 1)
            for c in range(CT):
                act.activation(a_dec[:, c, :], r_gate[:, c, :], ACT.Exp, scale=decay[:, 7, c:c + 1]).then_inc(a_ready, 1)
            for c in range(CT):
                act.wait_ge(rg_neg, c + 1)
                act.activation(r_gate[:, c, :], tanh_a[:, c, :], ACT.Sqrt, scale=-1.0).then_inc(rg_root, 1)
            g0 = SEG["gr"][0]
            for c in range(CT):
                hi(g0 + c + LOOK)
                act.wait_ge(pe_groups, g0 + c + 1)
                act.wait_ge(rg_step, 3 * (c + 1))
                act.activation(xc[:, c, :], psum[4 + c][:, :], ACT.Gelu_apprx_tanh).then_inc(gelu_ready, 1)
            g0 = SEG["v"][0]
            for c in range(CT):
                hi(g0 + c + LOOK)
            act.wait_ge(pe_groups, g0 + CT)
            act.wait_ge(q_ready, 2 * CT)
            act.wait_ge(rg_done, CT)
            for c in range(CT):
                act.activation(v_hi[:, c, :], psum[c][:, :], ACT.Copy).then_inc(vhi_ready, 1)
            steps = [0]

            def weights(u):
                h, i = UNITS[u]
                n = T - P * i
                act.wait_ge(expo_ready, u + 1)
                if u >= 2:
                    act.wait_ge(w_ready, u - 1)
                act.activation(w32[:, u % 2, 0:n], psum[u % 4][:, 0:n], ACT.Exp).then_inc(w32_ready, 1)

            for u, (h, i) in enumerate(UNITS):
                n = T - P * i
                act.wait_ge(z_ready, u + 1)
                if u >= 2:
                    act.wait_ge(l_ready, u - 1)
                for src, func, kw in ((psum[u % 4][:, 0:n], ACT.Abs, {}), (sp[:, u % 2, 0:n], ACT.Exp, {"scale": -1.0}),
                                      (sp[:, u % 2, 0:n], ACT.Ln, {"bias": one_col[:, :]})):
                    act.activation(sp[:, u % 2, 0:n], src, func, **kw).then_inc(lnx_step, 1)
                    steps[0] += 1
                    if func != ACT.Ln:
                        act.wait_ge(lnx_step, steps[0])
                if u >= 2:
                    weights(u - 2)
            weights(len(UNITS) - 2)
            weights(len(UNITS) - 1)
            act.wait_ge(o_ready, HEADS)
            act.dma_start(key32[:, :, :], keys).then_inc(keys_landed, 16)
            for n, t0 in ((8, 0), (9, CT)):
                norm(n, S2("out_gain", t0, CT), S2("zero2", 0, CT), h_split, o, t0)
            act.wait_ge(keys_landed, 16)
            act.activation(key_hi[:, :, :], key32[:, :, :], ACT.Copy).then_inc(keys_hi, 1)
            g0 = SEG["mix_out"][0]
            for c in range(KT):
                hi(g0 + c + LOOK)
            norm(10, S2("norm_ffn", 0, KT), S2("zero2", 0, KT), h_split)
            g0 = SEG["query"][0]
            for t in range(HP):
                hi(g0 + t + LOOK)
                act.wait_ge(pe_groups, g0 + t + 1)
                if t >= 2:
                    act.wait_ge(scores_done, t - 1)
                act.activation(qt_hi[:, t % 2, :], psum[t % 2][:, :], ACT.Copy).then_inc(qthi_ready, 1)
            up = SEG["up"][0]

            def store_acts(m, i):
                act.wait_ge(gelu_done, at(m + 1, i, 4))
                dst = expert_acts[m] if i is None else expert_acts[bass.ds(i * 4 + m, 1)].rearrange("a n t -> (a n) t")
                act.dma_start(dst, act_out[:, m % 4, :]).then_inc(acts_stored[m % 4], 16)

            def column(m, i):
                hi(up + m + LOOK, i, 4)
                act.wait_ge(pe_groups, at(up + m + 1, i, 4))
                if m >= 4:
                    act.wait_ge(acts_stored[m % 4], at(16 * (m // 4), i, 16))
                act.activation(act_out[:, m % 4, :], psum[4 + m % 4][:, :], ACT.Gelu_apprx_tanh).then_inc(gelu_done, 1)
                if m:
                    store_acts(m - 1, i)

            def columns_run(m0, n):
                if m0 == 0:
                    for m in range(4):
                        column(m, None)
                    m0, n = 4, n - 4
                with act.Fori(0, n // 4) as i:
                    for m in range(m0, m0 + 4):
                        column(m, i)

            def take_rows(c, i, cols):
                act.wait_ge(hot_used, at(c + 1, i, 4))
                for half in range(2):
                    k = cols + 4 * half
                    dst = spread[:, :, bass.ds(i * (4 * TC) + k, 4)]
                    act.activation(dst.rearrange("p m t -> p t m"), psum[2 * (c % 2) + half][:, :].rearrange("p (t m) -> p t m", t=4), ACT.Copy).then_inc(spread_ready, 1)

            for tt in range(TT):
                columns_run(tt * LEAD, LEAD)
                act.wait_ge(below_ready, tt + 1)
                act.activation(expo[:, :, :], below[:, :, :], ACT.Exp).then_inc(exp_ready, 1)
            for tt in range(TT):
                m0 = TT * LEAD + tt * (CHUNKS + GAP)
                if tt:
                    act.wait_ge(spilled, 16 * tt)
                with act.Fori(0, CHUNKS // 4) as i:
                    for k in range(4):
                        column(m0 + k, i)
                        take_rows(CHUNKS * tt + k, i, TC * k)
                act.wait_ge(spread_ready, 2 * CHUNKS * (tt + 1))
                act.dma_start(expert_weights[tt], spread[:, :, :]).then_inc(spilled, 16)
                columns_run(m0 + CHUNKS, GAP)
            store_acts(NK - 1, None)
            def load_column(m, i):
                s = m % 4
                if m >= 4:
                    act.wait_ge(we_mul, at(m - 3, i, 2 * MB))
                if i is None:
                    g, a = expert_weights[:, :, m, :].rearrange("a n t -> n a t"), expert_acts[m]
                else:
                    g = expert_weights[:, :, bass.ds(i * (2 * MB) + m, 1), :].rearrange("a n m t -> n a (m t)")
                    a = expert_acts[bass.ds(i * (2 * MB) + m, 1)].rearrange("a n t -> (a n) t")
                act.dma_start(g_ring[:, s, :].rearrange("p (a t) -> p a t", a=TT), g).then_inc(g_landed[s], 16)
                act.dma_start(act_in[:, s, :], a).then_inc(a_landed[s], 16)

            def out_step(b, i):
                for j in range(MB):
                    m = MB * b + j
                    if b:
                        hi(v_group(b - 1, j) + LOOK, i, 2 * MB)
                    if b < NB:
                        if m + 3 < NK:
                            load_column(m + 3, i)
                        act.wait_ge(we_mul, at(m + 1, i, 2 * MB))
                        if b >= 2 and j == 0:
                            act.wait_ge(pe_groups, at(v_group(b - 2, KT - 1) + 1, i, 2 * MB))
                        act.activation(we_hi[:, m % (2 * MB), :], we32[:, m % 2, :], ACT.Copy).then_inc(we_hi_ready, 1)

            act.wait_ge(spilled, 16 * TT)
            for k in range(4):
                act.wait_ge(acts_stored[k], 16 * NK // 4)
            for m in range(3):
                load_column(m, None)
            out_step(0, None)
            out_step(1, None)
            with act.Fori(0, NB // 2 - 2) as i:
                out_step(2, i)
                out_step(3, i)
            for b in range(NB - 2, NB + 1):
                out_step(b, None)

        @block.vector
        def _(dve):
            def ada_half(c, i=None, m=0):
                hf = c // 8 % 2
                acc = ada_accs[hf]
                for k in range(8):
                    u = c + k
                    if k == 0 and c >= 16:
                        dve.wait_ge(ada_summed, at(c // 16, i, m // 16))
                    dve.wait_ge(ada_landed[u % 4], at(16 * (u // 4 + 1), i, 4 * m))
                    if k:
                        dve.wait_ge(ada_used, at(u, i, m))
                        dve.scalar_tensor_tensor(acc[:, :], ada_raw[:, u % 4, :], cond[:, k:k + 1], acc[:, :],
                                                 ALU.mult, ALU.add).then_inc(ada_used, 1)
                    else:
                        dve.tensor_scalar(acc[:, :], ada_raw[:, u % 4, :], cond[:, k:k + 1], None,
                                          ALU.mult).then_inc(ada_used, 1)

            def ada_finish(it, i=None, m=0):
                dve.wait_ge(ada_summed, at(it + 1, i, m))
                cols = mod[:, it * KT:(it + 1) * KT] if i is None else mod[:, bass.ds(i * KT + it * KT, KT)]
                bias = S("ada_b", it * KT, KT) if i is None else small[:, bass.ds(i * KT + (SMALL["ada_b"] + it * KT), KT)]
                dve.tensor_tensor(cols, psum[6][:, 0:KT], bias, ALU.add).then_inc(mod_ready, 1)

            def coefficients(n, factor):
                dve.wait_ge(mod_ready, 3 * n + 3)
                sl = slice(n * KT, (n + 1) * KT)
                dve.scalar_tensor_tensor(coef[:, 0, sl], mod[:, (3 * n + 1) * KT:(3 * n + 2) * KT], 1.0,
                                         S("norm_g", n * KT, KT), ALU.add, ALU.mult).then_inc(coef_ready, 1)
                gate = mod[:, (3 * n + 2) * KT:(3 * n + 3) * KT]
                if isinstance(factor, float):
                    dve.tensor_scalar(coef[:, 1, sl], gate, factor, None, ALU.mult).then_inc(coef_ready, 1)
                else:
                    dve.tensor_tensor(coef[:, 1, sl], gate, factor, ALU.mult).then_inc(coef_ready, 1)

            def norm_sum(n):
                s0 = tiles_before(ALL_NORMS, n)
                for k in range(NORM_TILES[n]):
                    dve.wait_ge(sq_ready, s0 + k + 1)
                    if k:
                        dve.wait_ge(sq_used, s0 + k)
                        dve.tensor_tensor(sqsum[:, :], sqsum[:, :], sq[:, k % 2, :], ALU.add).then_inc(sq_used, 1)
                    else:
                        dve.tensor_copy(sqsum[:, :], sq[:, 0, :]).then_inc(sq_used, 1)
                dve.wait_ge(std_ready, n + 1)
                dve.reciprocal(rstd[:, :], std[:, :]).then_inc(rstd_ready, 1)
                dve.wait_ge(rstd_ready, n + 1)

            def norm(n, second, src=x, t0=0):
                norm_sum(n)
                for k in range(NORM_TILES[n] + 1):
                    if 2 <= k < NORM_TILES[n]:
                        if n == 1:
                            dve.wait_ge(pool_h, k - 1)
                        else:
                            dve.wait_ge(hhi_ready, tiles_before(SPLIT_NORMS, n) + k - 1)
                    if k < NORM_TILES[n]:
                        dve.tensor_tensor(xn[:, k % 2, :], src[:, t0 + k, :], rstd[:, :], ALU.mult).then_inc(xn_ready, 1)
                    if k:
                        second(n, k - 1)

            def h_low(n, k):
                dve.wait_ge(hhi_ready, tiles_before(SPLIT_NORMS, n) + k + 1)
                o_k = k + (4 if n == 9 else 0)
                dve.tensor_tensor(hlo[:, o_k, :], h32[:, k % 2, :], hhi[:, o_k, :].bitcast(F32), ALU.subtract).then_inc(h_ready, 1)

            def ffn(q):
                g0 = SEG[f"ffn{q}_in"][0]
                new = ADA_NEW[q]
                it0 = ADA_AT.get(q, 0)

                def tile(j, i):
                    g = g0 + 2 * j
                    t = FT * q + j
                    dve.wait_ge(silu_ready, at(t + 1, i, 2))
                    dve.wait_ge(pe_groups, at(g + 2, i, 4))
                    if t >= 2:
                        dve.wait_ge(uhi_ready, at(t - 1, i, 2))
                    dve.tensor_tensor(u32[:, j % 2, :], silu[:, j % 2, :], psum[2 * (j % 2) + 1][:, :],
                                      ALU.mult).then_inc(u_mul, 1)
                    dve.wait_ge(uhi_ready, at(t + 1, i, 2))
                    if i is None:
                        a, b = uhi[:, j, :], ulo[:, j, :]
                    else:
                        a, b = (z[:, bass.ds(i * 2 + j, 1), :].rearrange("p a t -> p (a t)") for z in (uhi, ulo))
                    dve.tensor_tensor(b, u32[:, j % 2, :], a.bitcast(F32), ALU.subtract).then_inc(u_ready, 1)

                def iteration(j, i, finish, units):
                    it = it0 + j // 2
                    tile(j, i)
                    if finish:
                        ada_finish(it - 1, i, 1)
                    if units:
                        ada_half(16 * it, i, 16)
                    tile(j + 1, i)
                    if units:
                        ada_half(16 * it + 8, i, 16)

                iteration(0, None, False, new > 0)
                if new > 1:
                    with dve.Fori(0, new - 1) as i:
                        iteration(2, i, True, True)
                last = max(new, 1)
                if new:
                    iteration(2 * last, None, True, False)
                    last += 1
                with dve.Fori(0, FT // 2 - last) as i:
                    iteration(2 * last, i, False, False)
                g1 = SEG[f"ffn{q}_out"][0]
                n = SUB_NORM[q]
                for half in range(2):
                    dve.wait_ge(pe_groups, g1 + (half + 1) * (FT // 2))
                    for d in range(4):
                        k = half * 4 + d
                        dve.scalar_tensor_tensor(x[:, k, :], psum[4 - 4 * half + d][:, :],
                                                 coef[:, 1, n * KT + k:n * KT + k + 1], x[:, k, :],
                                                 ALU.mult, ALU.add).then_inc(x_ready, 1)

            dve.memset(one_col[:, :], 1.0).then_inc(setup_done, 1)
            dve.wait_ge(const_landed, 64)
            dve.wait_ge(cond_ready, 1)
            for it in range(3):
                ada_half(16 * it)
                ada_half(16 * it + 8)
                if it:
                    ada_finish(it - 1)
            ada_finish(2)
            coefficients(0, 0.5)
            norm(0, h_low)
            ffn(0)
            dve.memset(pad0[:, :, 0:16], 0.0).then_inc(setup_done, 1)
            dve.wait_ge(setup_done, 2)
            coefficients(1, S("pool_scale", 0, KT))
            step = [0]

            def chained(ins):
                step[0] += 1
                ins.then_inc(pool_step, 1)
                dve.wait_ge(pool_step, step[0])

            def pool_mix(n, k):
                dve.wait_ge(pool_h, k + 1)
                if k:
                    dve.wait_ge(pool_mixed, k)
                w = 2 << (k // 2)
                src = pad0[:, k % 2, :]
                bufs, b, sft = [pad1, pad2], 0, 1
                while sft < w:
                    lo = 2 * sft - 1
                    dst = bufs[b]
                    chained(dve.tensor_tensor(dst[:, lo:16 + T], src[:, lo:16 + T], src[:, lo - sft:16 + T - sft], ALU.add))
                    src, b, sft = dst[:, :], 1 - b, 2 * sft
                if k >= 2:
                    dve.wait_ge(pool_hi, k - 1)
                chained(dve.tensor_tensor(src[:, 16:16 + w - 1], src[:, 16:16 + w - 1], corr[:, CORR[w]:CORR[w] + w - 1], ALU.mult))
                dve.scalar_tensor_tensor(mix32[:, k % 2, :], src[:, 16:16 + T], 1.0 / w, pad0[:, k % 2, 16:16 + T],
                                         ALU.mult, ALU.subtract).then_inc(pool_mixed, 1)
                if k:
                    pool_low(k - 1)

            def pool_low(k):
                dve.wait_ge(pool_hi, k + 1)
                dve.wait_ge(pool_mixed, k + 1)
                dve.tensor_tensor(hlo[:, k, :], mix32[:, k % 2, :], hhi[:, k, :].bitcast(F32), ALU.subtract).then_inc(pool_ready, 1)

            norm(1, pool_mix)
            pool_low(KT - 1)
            for k in range(KT):
                if k in (0, 4):
                    dve.wait_ge(pe_groups, SEG["pool"][0] + k // 4 + 1)
                dve.scalar_tensor_tensor(x[:, k, :], psum[k][:, :], coef[:, 1, KT + k:KT + k + 1], x[:, k, :],
                                         ALU.mult, ALU.add).then_inc(x_ready, 1)
            coefficients(2, 0.5)
            norm(2, h_low)
            ffn(1)
            coefficients(3, 0.5)
            norm(3, h_low)
            ffn(2)
            coefficients(4, 1.0)
            dve.memset(cu[:, :, 0:2], 0.0).then_inc(cv_step, 1)
            norm(4, h_low)
            g0 = SEG["conv_in"][0]
            cstep = [1]

            def cchained(ins):
                cstep[0] += 1
                ins.then_inc(cv_step, 1)
                dve.wait_ge(cv_step, cstep[0])

            dve.wait_ge(cv_step, 1)
            for j in range(KT):
                b = 3 * (j % 2)
                dve.wait_ge(cgate_ready, j + 1)
                dve.wait_ge(pe_groups, g0 + 3 * j + 2)
                dve.tensor_tensor(cu[:, j % 2, 2:2 + T], cgate[:, j % 2, :], psum[b + 1][:, :], ALU.mult).then_inc(cu_ready, 1)
                dve.wait_ge(cu_ready, j + 1)
                if j:
                    dve.wait_ge(y32_ready, j)
                cchained(dve.tensor_scalar(cv[:, 0, :], cu[:, j % 2, 2:2 + T], S("conv_w", 2 * KT + j), None, ALU.mult))
                cchained(dve.scalar_tensor_tensor(cv[:, 1, :], cu[:, j % 2, 1:1 + T], S("conv_w", KT + j), cv[:, 0, :], ALU.mult, ALU.add))
                cchained(dve.scalar_tensor_tensor(cv[:, 0, :], cu[:, j % 2, 0:T], S("conv_w", j), cv[:, 1, :], ALU.mult, ALU.add))
                dve.wait_ge(pe_groups, g0 + 3 * j + 3)
                dve.tensor_tensor(y32[:, j % 2, :], cv[:, 0, :], psum[b + 2][:, :], ALU.mult).then_inc(y32_ready, 1)
                dve.wait_ge(yhi_ready, j + 1)
                dve.tensor_tensor(ylo[:, j, :], y32[:, j % 2, :], yhi[:, j, :].bitcast(F32), ALU.subtract).then_inc(y_ready, 1)
            g0 = SEG["conv_out"][0]
            for k in range(KT):
                dve.wait_ge(pe_groups, g0 + k + 1)
                dve.scalar_tensor_tensor(x[:, k, :], psum[k][:, :], coef[:, 1, 4 * KT + k:4 * KT + k + 1], x[:, k, :],
                                         ALU.mult, ALU.add).then_inc(x_ready, 1)
            coefficients(5, 0.5)
            norm(5, h_low)
            ffn(3)
            norm_sum(6)
            for k in range(KT):
                dve.scalar_tensor_tensor(x[:, k, :], x[:, k, :], S("final_g", k), rstd[:, :],
                                         ALU.mult, ALU.mult).then_inc(x_ready, 1)
            dve.wait_ge(const2_landed, 48)
            dstep = [0]

            def dchained(ins):
                dstep[0] += 1
                ins.then_inc(decay_step, 1)
                dve.wait_ge(decay_step, dstep[0])

            def dk(j):
                return decay[:, j, 0:CT]

            dve.memset(xpad[:, :, 0:8], 0.0).then_inc(setup_done, 1)
            dchained(dve.scalar_tensor_tensor(dk(0), S2("lam", 0, CT), -1.0, S2("lam", 0, CT), ALU.mult, ALU.max))
            dve.wait_ge(decay_exp, 1)
            dchained(dve.tensor_scalar(dk(2), dk(1), 2.0, None, ALU.add))
            dchained(dve.reciprocal(dk(3), dk(2)))
            dchained(dve.tensor_tensor(dk(2), dk(1), dk(3), ALU.mult))
            dchained(dve.tensor_tensor(dk(3), dk(2), dk(2), ALU.mult))
            dchained(dve.tensor_scalar(dk(4), dk(3), 1.0 / 17, None, ALU.mult))
            for q in (15, 13, 11, 9, 7, 5, 3):
                dchained(dve.scalar_tensor_tensor(dk(4), dk(4), 1.0 / q, dk(3), ALU.add, ALU.mult))
            dchained(dve.scalar_tensor_tensor(dk(5), dk(4), 1.0, dk(2), ALU.add, ALU.mult))
            dchained(dve.tensor_scalar(dk(6), S2("lam", 0, CT), -1.0, 0.0, ALU.mult, ALU.max))
            dchained(dve.scalar_tensor_tensor(dk(4), dk(5), 2.0, dk(6), ALU.mult, ALU.add))
            dchained(dve.tensor_scalar(dk(7), dk(4), -8.0, None, ALU.mult))
            dchained(dve.tensor_scalar(dk(5)[:, 0:1], S2("q_gain"), 0.125, None, ALU.mult))
            assert dstep[0] == DECAY_STEPS
            norm(7, h_low)
            xstep = [0]

            def xchained(ins):
                xstep[0] += 1
                ins.then_inc(conv2_step, 1)
                dve.wait_ge(conv2_step, xstep[0])

            dve.wait_ge(setup_done, 3)
            for c in range(CT):
                dve.wait_ge(xpad_ready, c + 1)
                row = xpad[:, c % 2, :]
                xchained(dve.tensor_scalar(cx[:, 0, :], row[:, 8:8 + T], S2("conv_w2", 3 * CT + c), S2("conv_b2", c), ALU.mult, ALU.add))
                xchained(dve.scalar_tensor_tensor(cx[:, 1, :], row[:, 7:7 + T], S2("conv_w2", 2 * CT + c), cx[:, 0, :], ALU.mult, ALU.add))
                xchained(dve.scalar_tensor_tensor(cx[:, 0, :], row[:, 6:6 + T], S2("conv_w2", CT + c), cx[:, 1, :], ALU.mult, ALU.add))
                dve.scalar_tensor_tensor(xc[:, c, :], row[:, 5:5 + T], S2("conv_w2", c), cx[:, 0, :], ALU.mult, ALU.add).then_inc(xc_ready, 1)
                dve.wait_ge(xc_ready, c + 1)
                dve.wait_ge(xc_hi_ready, c + 1)
                dve.tensor_tensor(xc_lo[:, c, :], xc[:, c, :], xc_hi[:, c, :].bitcast(F32), ALU.subtract).then_inc(xc_lo_ready, 1)

            def q_low(t):
                dve.wait_ge(qhi_ready, t + 1)
                a, b = (q_hi, q_lo) if t < CT else (k_hi, k_lo)
                dve.tensor_tensor(b[:, t % CT, :], qn[:, t % 2, :], a[:, t % CT, :].bitcast(F32), ALU.subtract).then_inc(q_ready, 1)

            for t in range(2 * CT):
                dve.wait_ge(qstd_ready, t + 1)
                if t:
                    dve.wait_ge(qn_ready, t)
                dve.reciprocal(qrstd[:, :], qstd[:, :]).then_inc(qrstd_ready, 1)
                dve.wait_ge(qrstd_ready, t + 1)
                if t >= 2:
                    dve.wait_ge(q_ready, t - 1)
                gain = dk(5)[:, 0:1] if t < CT else S2("k_gain")
                dve.scalar_tensor_tensor(qn[:, t % 2, :], psum[4 + t % 2][:, :], gain, qrstd[:, :], ALU.mult, ALU.mult).then_inc(qn_ready, 1)
                if t:
                    q_low(t - 1)
            q_low(2 * CT - 1)
            for c in range(CT):
                dve.wait_ge(gates_ready, 2 * c + 2)
                dve.tensor_tensor(i_gate[:, c, :], i_gate[:, c, :], xc[:, c, :], ALU.mult).then_inc(rg_step, 1)
                dve.wait_ge(a_ready, c + 1)
                dve.tensor_tensor(r_gate[:, c, :], a_dec[:, c, :], a_dec[:, c, :], ALU.mult).then_inc(rg_step, 1)
                dve.wait_ge(rg_step, 3 * c + 2)
                dve.scalar_tensor_tensor(tanh_a[:, c, :], r_gate[:, c, :], 1.0, tanh_a[:, c, :], ALU.add, ALU.mult).then_inc(rg_neg, 1)
                dve.wait_ge(rg_root, c + 1)
                dve.tensor_tensor(i_gate[:, c, :], i_gate[:, c, :], r_gate[:, c, :], ALU.mult).then_inc(rg_step, 1)
                dve.wait_ge(rg_step, 3 * c + 3)
                dve.tensor_tensor_scan(o[:, CT + c, :], a_dec[:, c, :], i_gate[:, c, :], 0.0, ALU.mult, ALU.add).then_inc(rg_done, 1)
            for c in range(CT):
                dve.wait_ge(gelu_ready, c + 1)
                dve.wait_ge(rg_done, c + 1)
                dve.tensor_tensor(o[:, CT + c, :], o[:, CT + c, :], xc[:, c, :], ALU.mult).then_inc(rg_out, 1)
            for c in range(CT):
                dve.wait_ge(vhi_ready, c + 1)
                dve.tensor_tensor(v_lo[:, c, :], psum[c][:, :], v_hi[:, c, :].bitcast(F32), ALU.subtract).then_inc(v_ready, 1)
            lsteps = [0]

            def split_w(u):
                h, i = UNITS[u]
                n = T - P * i
                dve.wait_ge(w32_ready, u + 1)
                if u >= 2:
                    dve.wait_ge(pv_done, u - 1)
                dve.tensor_copy(w_hi[:, u % 2, 0:n], w32[:, u % 2, 0:n]).then_inc(whi_ready, 1)
                dve.wait_ge(whi_ready, u + 1)
                dve.tensor_tensor(w_lo[:, u % 2, 0:n], w32[:, u % 2, 0:n], w_hi[:, u % 2, 0:n].bitcast(F32), ALU.subtract).then_inc(w_ready, 1)
                if i == 0 and h:
                    take_o(h - 1)

            def take_o(h):
                dve.wait_ge(pv_done, CT * (h + 1))
                rows = slice(64 * (h % 2), 64 * (h % 2) + 64)
                dve.tensor_copy(o[rows, h // 2, :], psum[4 + h % 2][rows, :]).then_inc(o_ready, 1)

            for u, (h, i) in enumerate(UNITS):
                n = T - P * i
                buf, cols = sp[:, u % 2, 0:n], slice(ATT_OFF[i], ATT_OFF[i] + n)
                dve.wait_ge(lnx_step, 3 * (u + 1))
                dve.scalar_tensor_tensor(buf, psum[u % 4][:, 0:n], 0.0, buf, ALU.max, ALU.add).then_inc(sp_ready, 1)
                dve.wait_ge(sp_ready, 2 * u + 1)
                dve.tensor_tensor(sp[:, u % 2, 0:P], sp[:, u % 2, 0:P], sq_plain[:, MASK, :], ALU.mult).then_inc(sp_ready, 1)
                dve.wait_ge(sp_ready, 2 * u + 2)
                if h >= 2:
                    dve.wait_ge(expo_ready, CT * (h - 1))
                dve.tensor_copy(l_hi[:, h % 2, cols], buf).then_inc(lhi_ready, 1)
                dve.wait_ge(lhi_ready, u + 1)
                dve.tensor_tensor(l_lo[:, h % 2, cols], buf, l_hi[:, h % 2, cols].bitcast(F32), ALU.subtract).then_inc(l_ready, 1)
                if u >= 2:
                    split_w(u - 2)
            split_w(len(UNITS) - 2)
            split_w(len(UNITS) - 1)
            take_o(HEADS - 1)
            for n, t0 in ((8, 0), (9, CT)):
                norm(n, h_low, o, t0)
            dve.wait_ge(keys_hi, 1)
            dve.tensor_tensor(key_lo[:, :, :], key32[:, :, :], key_hi[:, :, :].bitcast(F32), ALU.subtract).then_inc(keys_ready, 1)
            g0 = SEG["mix_out"][0]
            for k in range(KT):
                dve.wait_ge(pe_groups, g0 + k + 1)
                dve.tensor_tensor(x[:, k, :], psum[k][:, :], x[:, k, :], ALU.add).then_inc(x_ready, 1)
            dve.tensor_copy(iota_b[:, :], sq_plain[:, IOTA, :]).then_inc(iota_ready, 1)
            norm(10, h_low)
            tops = [0]

            def tops_done():
                dve.wait_ge(top_step, tops[0])

            def top(ins):
                tops[0] += 1
                ins.then_inc(top_step, 1)

            def best_keys(t):
                h, half = t // 2, t % 2
                dve.wait_ge(scores_done, t + 1)
                s = [psum[2 + t % 2][:, tt * P:(tt + 1) * P] for tt in range(TT)]
                v, ix = top_v[:, h, half, :, :], top_i[:, h, half, :, :]
                for tt in range(TT):
                    top(dve.max(v[:, tt, 0:8], s[tt]))
                tops_done()
                for tt in range(TT):
                    top(dve.match_replace(rest1[:, tt, :], v[:, tt, 0:8], s[tt], LOWEST))
                    top(dve.max_index(ix[:, tt, 0:8], v[:, tt, 0:8], s[tt]))
                tops_done()
                for tt in range(TT):
                    top(dve.max(v[:, tt, 8:16], rest1[:, tt, :]))
                tops_done()
                for tt in range(TT):
                    top(dve.max_index(ix[:, tt, 8:16], v[:, tt, 8:16], rest1[:, tt, :]))
                assert tops[0] == 5 * TT * (t + 1)

            for t in range(HP + 1):
                if t < HP:
                    dve.wait_ge(qthi_ready, t + 1)
                    dve.tensor_tensor(qt_lo[:, t % 2, :], psum[t % 2][:, :], qt_hi[:, t % 2, :].bitcast(F32), ALU.subtract).then_inc(qt_ready, 1)
                if t:
                    tops_done()
                    best_keys(t - 1)
            tops_done()
            steps = [0]

            def sel(ins):
                steps[0] += 1
                ins.then_inc(sel_step, 1)

            def seld():
                dve.wait_ge(sel_step, steps[0])

            sel(dve.tensor_copy(top_b[:, :, :, :, :], top_i[:, :, :, :, :]))
            dve.wait_ge(iota_ready, 1)

            def best_pairs(tt):
                grid = [P, PH, TOP, TOP]
                seld()
                sel(dve.tensor_tensor(cand[:, :, :].rearrange("p h (a b) -> p h a b", a=TOP),
                                      top_v[:, :, 0, tt, :].unsqueeze(3).to_broadcast(grid),
                                      top_v[:, :, 1, tt, :].unsqueeze(2).to_broadcast(grid), ALU.add))
                seld()
                for h in range(PH):
                    sel(dve.max(best_v[:, h, 0:8], cand[:, h, :]))
                seld()
                for h in range(PH):
                    sel(dve.match_replace(rest2[:, h, :], best_v[:, h, 0:8], cand[:, h, :], LOWEST))
                    sel(dve.max_index(best_p[:, h, 0:8], best_v[:, h, 0:8], cand[:, h, :]))
                seld()
                for h in range(PH):
                    sel(dve.max(best_v[:, h, 8:16], rest2[:, h, :]))
                seld()
                dve.tensor_tensor(below[:, :, :], best_v[:, :, :], best_v[:, :, 0:1].to_broadcast([P, PH, TOP]), ALU.subtract).then_inc(below_ready, 1)
                for h in range(PH):
                    sel(dve.max_index(best_p[:, h, 8:16], best_v[:, h, 8:16], rest2[:, h, :]))
                seld()
                sel(dve.tensor_scalar(pos_u[:, 0, :, :], best_p[:, :, :], 4, None, ALU.logical_shift_right))
                sel(dve.tensor_scalar(pos_u[:, 1, :, :], best_p[:, :, :], 15, None, ALU.bitwise_and))
                seld()
                sel(dve.tensor_copy(pos_b[:, :, :, :], pos_u[:, :, :, :]))
                seld()
                for half in range(2):
                    sel(dve.tensor_tensor(is_pos[:, :, :, :], iota_b[:, 0:TOP].unsqueeze(1).unsqueeze(1).to_broadcast(grid),
                                          pos_b[:, half, :, :].unsqueeze(3).to_broadcast(grid), ALU.is_equal))
                    seld()
                    sel(dve.tensor_tensor(prod[:, :, :, :], is_pos[:, :, :, :],
                                          top_b[:, :, half, tt, :].unsqueeze(2).to_broadcast(grid), ALU.mult))
                    seld()
                    if half == 0 and tt:
                        dve.wait_ge(turned, tt)
                    sel(dve.tensor_reduce(chosen[:, half, :].rearrange("p (h r) -> p h r", h=PH), prod[:, :, :, :], AXX, ALU.add))
                    seld()
                dve.wait_ge(exp_ready, tt + 1)
                sel(dve.tensor_reduce(esum[:, 0, :], expo[:, :, :], AXX, ALU.add))
                seld()
                sel(dve.reciprocal(esum[:, 1, :], esum[:, 0, :]))
                seld()
                dve.tensor_tensor(chosen[:, 2, :].rearrange("p (h r) -> p h r", h=PH), expo[:, :, :],
                                  esum[:, 1, :].unsqueeze(2).to_broadcast([P, PH, TOP]), ALU.mult).then_inc(chosen_ready, 1)

            picks = [0]

            def pk(ins):
                picks[0] += 1
                ins.then_inc(pick_step, 1)
                dve.wait_ge(pick_step, picks[0])

            def take_turned(tt):
                cols = slice(tt * P, (tt + 1) * P)
                dve.wait_ge(turned, tt + 1)
                w = psum[0][:, 2 * P:3 * P]
                pk(dve.tensor_copy(pick[:, 0:2, cols], psum[0][:, 0:2 * P].rearrange("p (a t) -> p a t", a=2)))
                pk(dve.tensor_copy(pick[:, 2, cols], w))
                pk(dve.tensor_tensor(left[:, 0, :], w, pick[:, 2, cols], ALU.subtract))
                pk(dve.tensor_copy(pick[:, 3, cols], left[:, 0, :]))
                pk(dve.tensor_tensor(left[:, 1, :], left[:, 0, :], pick[:, 3, cols], ALU.subtract))
                pk(dve.tensor_copy(pick[:, 4, cols], left[:, 1, :]))

            for tt in range(TT):
                best_pairs(tt)
                take_turned(tt)
            def rows(c, i):
                s = c % 2
                if c >= 2:
                    dve.wait_ge(hot_used, at(c - 1, i, 4))
                    dve.wait_ge(hot_third, at(c - 1, i, 4))
                numbers = iota_b[:, :].unsqueeze(1).to_broadcast([P, TC, P])
                dve.tensor_tensor(hot_m[:, s, :, :], numbers, hot_column(1, c, i), ALU.is_equal).then_inc(hot_mark, 1)
                dve.tensor_tensor(hot_n[:, s, :, :], numbers, hot_column(0, c, i), ALU.is_equal).then_inc(hot_ready, 1)
                dve.wait_ge(hot_mark, at(c + 1, i, 4))
                for part in range(2):
                    dve.tensor_tensor(hot_w[:, s, part, :, :], hot_m[:, s, :, :], hot_column(2 + part, c, i), ALU.mult).then_inc(hot_ready, 1)

            for c in range(4):
                rows(c, None)
            with dve.Fori(0, T // TC // 4 - 1) as i:
                for c in range(4, 8):
                    rows(c, i)
            def out_step(b, i):
                for j in range(MB):
                    m = MB * b + j
                    if b < NB:
                        dve.wait_ge(g_landed[m % 4], at(16 * (m // 4 + 1), i, 16 * 2 * MB // 4))
                        dve.wait_ge(a_landed[m % 4], at(16 * (m // 4 + 1), i, 16 * 2 * MB // 4))
                        if m >= 2:
                            dve.wait_ge(we_ready, at(m - 1, i, 2 * MB))
                        dve.tensor_tensor(we32[:, m % 2, :], act_in[:, m % 4, :], g_ring[:, m % 4, :], ALU.mult).then_inc(we_mul, 1)
                        dve.wait_ge(we_hi_ready, at(m + 1, i, 2 * MB))
                        if b >= 2 and j == 0:
                            dve.wait_ge(pe_groups, at(v_group(b - 2, KT - 1) + 1, i, 2 * MB))
                        dve.tensor_tensor(we_lo[:, m % (2 * MB), :], we32[:, m % 2, :], we_hi[:, m % (2 * MB), :].bitcast(F32),
                                          ALU.subtract).then_inc(we_ready, 1)
                    if b:
                        dve.wait_ge(pe_groups, at(v_group(b - 1, j) + 1, i, 2 * MB))
                        if b >= 2:
                            dve.wait_ge(y_added, at(KT * (b - 2) + j + 1, i, 2 * KT))
                        dve.tensor_tensor(x[:, j, :], psum[j][:, :], x[:, j, :], ALU.add).then_inc(y_added, 1)

            out_step(0, None)
            out_step(1, None)
            with dve.Fori(0, NB // 2 - 1) as i:
                out_step(2, i)
                out_step(3, i)
            out_step(NB, None)

        @block.tensor
        def _(pe):
            def three(bank, s, b, rhi, rlo, start, stop, last=None):
                pe.matmul(bank, whi[:, s, b, :], rhi, start=start, stop=False)
                pe.matmul(bank, whi[:, s, b, :], rlo, start=False, stop=False)
                return pe.matmul(bank, wlo[:, s, b, :], rhi, start=False, stop=stop)

            def row_group(bank, c, i=None, m=0, hi=None, lo=None, first=None, ready=h_ready):
                hi = hhi if hi is None else hi
                lo = hlo if lo is None else lo
                pe.wait_ge(lo_ready, at(c + 1, i, m))
                for k in range(GB):
                    if first is not None:
                        pe.wait_ge(ready, first + k + 1)
                    mm = three(bank, c % R, k, hi[:, k, :], lo[:, k, :], k == 0, k == GB - 1)
                mm.then_inc(pe_groups, 1)

            def ada_sums(it, i=None, m=0):
                pe.wait_ge(ada_used, at(16 * (it + 1), i, 16 * m))
                if it:
                    pe.wait_ge(mod_ready, at(it, i, m))
                for c in range(KT):
                    acc = ada_accs[c // 4]
                    mm = pe.matmul(psum[6][:, c:c + 1], acc[:, (c % 4) * P:(c % 4 + 1) * P], one_col[:, :], start=True, stop=True)
                mm.then_inc(ada_summed, 1)

            def mean_square(n):
                pe.wait_ge(sq_used, tiles_before(ALL_NORMS, n) + NORM_TILES[n])
                weights = sq_plain[:, MEAN_H, :] if n in (8, 9) else mean_d[:, :]
                pe.matmul(psum[7][:, :], weights, sqsum[:, :], start=True, stop=True).then_inc(ms_ready, 1)

            def ffn(q, h_first):
                g0 = SEG[f"ffn{q}_in"][0]
                new = ADA_NEW[q]
                it0 = ADA_AT.get(q, 0)

                def tile(j, i, first=None):
                    t = FT * q + j
                    if j >= 2:
                        pe.wait_ge(u_mul, at(t - 1, i, 2))
                    row_group(psum[2 * (j % 2)][:, :], g0 + 2 * j, i, 4, first=first)
                    row_group(psum[2 * (j % 2) + 1][:, :], g0 + 2 * j + 1, i, 4)

                tile(0, None, h_first)
                tile(1, None)
                if new > 1:
                    with pe.Fori(0, new - 1) as i:
                        tile(2, i)
                        ada_sums(it0, i, 1)
                        tile(3, i)
                last = max(new, 1)
                if new:
                    tile(2 * last, None)
                    ada_sums(it0 + new - 1)
                    tile(2 * last + 1, None)
                    last += 1
                with pe.Fori(0, FT // 2 - last) as i:
                    tile(2 * last, i)
                    tile(2 * last + 1, i)
                if new:
                    pe.wait_ge(mod_ready, it0 + new)
                g1 = SEG[f"ffn{q}_out"][0]

                def out_group(half, f, i):
                    c = g1 + half * (FT // 2) + f
                    pe.wait_ge(lo_ready, at(c + 1, i, 4))
                    pe.wait_ge(u_ready, at(FT * q + 2 * f + 2, i, 8))
                    for a in range(2):
                        if i is None:
                            rh, rl = uhi[:, 2 * f + a, :], ulo[:, 2 * f + a, :]
                        else:
                            rh, rl = (z[:, bass.ds(i * 8 + 2 * f + a, 1), :].rearrange("p a t -> p (a t)") for z in (uhi, ulo))
                        for d in range(4):
                            mm = three(psum[4 - 4 * half + d][:, :], c % R, a * 4 + d, rh, rl,
                                       f == 0 and a == 0, i is None and f == FT // 2 - 1 and a == 1)
                    mm.then_inc(pe_groups, 1)

                for half in range(2):
                    if half:
                        pe.wait_ge(u_mul, FT * (q + 1))
                    out_group(half, 0, None)
                    with pe.Fori(0, 2) as i:
                        for f in range(1, 5):
                            out_group(half, f, i)
                    out_group(half, 9, None)
                    out_group(half, 10, None)

            pe.wait_ge(const_landed, 64)
            pe.wait_ge(setup_done, 1)
            for it in range(3):
                ada_sums(it)
            mean_square(0)
            ffn(0, 0)
            mean_square(1)
            for g in range(4):
                c = SEG["pool"][0] + g // 2
                if g % 2 == 0:
                    pe.wait_ge(lo_ready, c + 1)
                pe.wait_ge(pool_ready, 2 * g + 2)
                for o in range(2):
                    for k in range(2):
                        mm = three(psum[2 * g + o][:, :], c % R, (g % 2) * 4 + o * 2 + k, hhi[:, 2 * g + k, :], hlo[:, 2 * g + k, :],
                                   k == 0, k == 1)
                if g % 2:
                    mm.then_inc(pe_groups, 1)
            mean_square(2)
            ffn(1, KT)
            mean_square(3)
            ffn(2, 2 * KT)
            mean_square(4)
            g0 = SEG["conv_in"][0]
            for j in range(KT):
                for part in range(3):
                    if j >= 2 and part == 0:
                        pe.wait_ge(y32_ready, j - 1)
                    row_group(psum[3 * (j % 2) + part][:, :], g0 + 3 * j + part, first=3 * KT if j == 0 and part == 0 else None)
            g0 = SEG["conv_out"][0]
            for k in range(KT):
                row_group(psum[k][:, :], g0 + k, hi=yhi, lo=ylo, first=0 if k == 0 else None, ready=y_ready)
            mean_square(5)
            ffn(3, 4 * KT)
            mean_square(6)
            mean_square(7)
            g0 = SEG["xr"][0]
            for c in range(CT):
                row_group(psum[c][:, :], g0 + c, first=5 * KT if c == 0 else None)
            g0 = SEG["qk"][0]

            def q_mean(t):
                pe.wait_ge(qsq_ready, t + 1)
                pe.matmul(psum[6 + t % 2][:, :], sq_plain[:, BLK, :], qsq[:, t % 2, :], start=True, stop=True).then_inc(qms_ready, 1)

            for t in range(2 * CT):
                if t >= 2:
                    pe.wait_ge(qn_ready, t - 1)
                row_group(psum[4 + t % 2][:, :], g0 + t)
                if t:
                    q_mean(t - 1)
            q_mean(2 * CT - 1)
            c0 = SEG["gates"][0]
            pe.wait_ge(lo_ready, c0 + 1)
            for c in range(CT):
                pe.wait_ge(xc_lo_ready, c + 1)
                if c >= 2:
                    pe.wait_ge(gates_ready, 2 * c - 2)
                for part in range(2):
                    mm = three(psum[2 * (c % 2) + part][:, :], c0 % R, 2 * c + part, xc_hi[:, c, :], xc_lo[:, c, :], True, True)
                mm.then_inc(gate_products if c < CT - 1 else pe_groups, 1)
            g0 = SEG["gr"][0]
            pe.wait_ge(qn_ready, 2 * CT)
            for c in range(CT):
                row_group(psum[4 + c][:, :], g0 + c)
            g0 = SEG["v"][0]
            pe.wait_ge(gates_ready, 2 * CT)
            for c in range(CT):
                s = (g0 + c) % R
                pe.wait_ge(lo_ready, g0 + c + 1)
                for a in range(2):
                    k = 2 * c + a
                    rh, rl = (w[:, s, 4 * a:4 * a + 4, :].rearrange("p b n -> p (b n)") for w in (whi, wlo))
                    for st in range(CT):
                        cols = slice(st * P, st * P + P)
                        pe.matmul(psum[st][:, :], hhi[:, k, cols], rh, start=k == 0, stop=False)
                        pe.matmul(psum[st][:, :], hlo[:, k, cols], rh, start=False, stop=False)
                        mm = pe.matmul(psum[st][:, :], hhi[:, k, cols], rl, start=False, stop=k == KT - 1)
                mm.then_inc(pe_groups, 1)
            def scores(u):
                h, i = UNITS[u]
                n = T - P * i
                if u >= 4:
                    pe.wait_ge(w32_ready, u - 3)
                r, t = slice(64 * (h % 2), 64 * (h % 2) + 64), h // 2
                out = psum[u % 4][:, 0:n]
                kc, qc = slice(P * i, P * i + P), slice(P * i, T)
                pe.matmul(out, k_hi[r, t, kc], q_hi[r, t, qc], start=True, stop=False)
                pe.matmul(out, k_hi[r, t, kc], q_lo[r, t, qc], start=False, stop=False)
                pe.matmul(out, k_lo[r, t, kc], q_hi[r, t, qc], start=False, stop=True).then_inc(z_ready, 1)

            def exponent(u):
                h, i = UNITS[u]
                pe.wait_ge(l_ready, u + 1)
                for j in range(i, CT):
                    off = P * (j - i)
                    n = T - P * j
                    out = psum[u % 4][:, off:off + n]
                    for part in (l_hi, l_lo):
                        pe.matmul(out, sq_round[:, TRI if j == i else ONES, :], part[:, h % 2, ATT_OFF[j]:ATT_OFF[j] + n],
                                  start=False, stop=False, skip_group_check=True)
                pe.matmul(psum[u % 4][:, 0:P], sq_round[:, IDENT_R, :], sq_round[:, FAR, :],
                          start=False, stop=True, skip_group_check=True).then_inc(expo_ready, 1)

            def weighted(u):
                h, i = UNITS[u]
                n = T - P * i
                pe.wait_ge(w_ready, u + 1)
                if i == CT - 1 and h >= 2:
                    pe.wait_ge(o_ready, h - 1)
                out = psum[4 + h % 2][:, P * i:T]
                fc = slice(P * (h // 2), P * (h // 2) + P)
                pe.matmul(out, v_hi[:, i, fc], w_hi[:, u % 2, 0:n], start=i == CT - 1, stop=False, skip_group_check=True)
                pe.matmul(out, v_hi[:, i, fc], w_lo[:, u % 2, 0:n], start=False, stop=False, skip_group_check=True)
                pe.matmul(out, v_lo[:, i, fc], w_hi[:, u % 2, 0:n], start=False, stop=i == 0, skip_group_check=True).then_inc(pv_done, 1)

            pe.wait_ge(q_ready, 2 * CT)
            pe.wait_ge(const2_ready, 1)
            pe.wait_ge(v_ready, CT)
            pe.wait_ge(rg_out, CT)
            for u in range(len(UNITS) + 3):
                if u < len(UNITS):
                    scores(u)
                if 2 <= u < len(UNITS) + 2:
                    exponent(u - 2)
                if u >= 3:
                    weighted(u - 3)
            mean_square(8)
            mean_square(9)
            g0 = SEG["mix_out"][0]
            pe.wait_ge(h_ready, tiles_before(SPLIT_NORMS, 10))
            for k in range(KT):
                row_group(psum[k][:, :], g0 + k)
            mean_square(10)

            def keyed_scores(t):
                pe.wait_ge(qt_ready, t + 1)
                if t >= 2:
                    pe.wait_ge(top_step, 5 * TT * (t - 1))
                for tt in range(TT):
                    cols = slice(tt * P, (tt + 1) * P)
                    out = psum[2 + t % 2][:, cols]
                    pe.matmul(out, qt_hi[:, t % 2, cols], key_hi[:, t, :], start=True, stop=False)
                    pe.matmul(out, qt_hi[:, t % 2, cols], key_lo[:, t, :], start=False, stop=False)
                    mm = pe.matmul(out, qt_lo[:, t % 2, cols], key_hi[:, t, :], start=False, stop=True)
                mm.then_inc(scores_done, 1)

            g0 = SEG["query"][0]
            pe.wait_ge(keys_ready, 1)
            for t in range(HP + 1):
                if t < HP:
                    if t >= 2:
                        pe.wait_ge(qt_ready, t - 1)
                    row_group(psum[t % 2][:, :], g0 + t, first=tiles_before(SPLIT_NORMS, 10) if t == 0 else None)
                if t:
                    keyed_scores(t - 1)
            up = SEG["up"][0]

            def column(m, i):
                if m >= 4:
                    pe.wait_ge(gelu_done, at(m - 3, i, 4))
                row_group(psum[4 + m % 4][:, :], up + m, i, 4)

            def columns_run(m0, n):
                if m0 == 0:
                    for m in range(4):
                        column(m, None)
                    m0, n = 4, n - 4
                with pe.Fori(0, n // 4) as i:
                    for m in range(m0, m0 + 4):
                        column(m, i)

            def sums(c, i):
                s = c % 2
                pe.wait_ge(hot_ready, at(3 * (c + 1), i, 12))
                pe.wait_ge(hot_third, at(c + 1, i, 4))
                if c >= 2:
                    pe.wait_ge(spread_ready, at(2 * (c - 1), i, 8))
                for k in range(TC):
                    out = psum[2 * s + k // 4][:, (k % 4) * P:(k % 4 + 1) * P]
                    for part in range(3):
                        mm = pe.matmul(out, hot_n[:, s, k, :], hot_w[:, s, part, k, :], start=part == 0, stop=part == 2)
                mm.then_inc(hot_used, 1)

            for tt in range(TT):
                columns_run(tt * LEAD, LEAD)
                pe.wait_ge(chosen_ready, tt + 1)
                if tt:
                    pe.wait_ge(pick_step, 6 * tt)
                for part in range(3):
                    mm = pe.matmul(psum[0][:, part * P:(part + 1) * P], chosen[:, part, :], sq_plain[:, IDENT, :], start=True, stop=True)
                mm.then_inc(turned, 1)
            for tt in range(TT):
                m0 = TT * LEAD + tt * (CHUNKS + GAP)
                c0 = tt * CHUNKS
                if tt == 0:
                    for k in range(4):
                        column(m0 + k, None)
                        sums(c0 + k, None)
                    m0, c0 = m0 + 4, c0 + 4
                with pe.Fori(0, CHUNKS // 4 - (tt == 0)) as i:
                    for k in range(4):
                        column(m0 + k, i)
                        sums(c0 + k, i)
                columns_run(TT * LEAD + tt * (CHUNKS + GAP) + CHUNKS, GAP)
            def down(b, i):
                pe.wait_ge(we_ready, at(MB * (b + 1), i, 2 * MB))
                k0 = MB * (b % 2)
                for d in range(KT):
                    if b:
                        pe.wait_ge(y_added, at(KT * (b - 1) + d + 1, i, 2 * KT))
                    row_group(psum[d][:, :], v_group(b, d), i, 2 * MB,
                              hi=we_hi[:, k0:k0 + MB, :], lo=we_lo[:, k0:k0 + MB, :])

            pe.wait_ge(spread_ready, 2 * T // TC)
            pe.wait_ge(gelu_done, NK)
            down(0, None)
            down(1, None)
            with pe.Fori(0, NB // 2 - 1) as i:
                down(2, i)
                down(3, i)


def columns(v):
    return np.ascontiguousarray(np.asarray(v).reshape(-1, P).T)


def rows_as_groups(w):
    w = np.asarray(w)
    n = w.shape[1] // P
    return w.reshape(KT, P, n, P).transpose(2, 1, 0, 3)


def layout(x, c, ada_w, ada_b, norm_g, ffn_w_in, ffn_w_out, pool_w, pool_scale, conv_w_in, conv_w, conv_w_out, final_g,
           norm_mix_2, w_in_2, q_norm_2, k_norm_2, conv_w_2, conv_b_2, rg_w_a_2, rg_b_a_2, rg_w_x_2, rg_b_x_2, rg_lambda_2,
           out_norm_sb_2, out_norm_rg_2, w_out_2, norm_ffn_2, peer_w_query_2, peer_sub_keys_2, peer_u_2, peer_v_2):
    A = np.asarray
    parts = []

    def ffn(l, s):
        g = rows_as_groups(A(ffn_w_in)[l, s])
        parts.append(np.stack([g[:FT], g[FT:]], 1).reshape(2 * FT, P, GB, P))
        w = A(ffn_w_out)[l, s].reshape(FT // 2, 2, P, 2, 4, P)
        parts.append(w.transpose(3, 0, 2, 1, 4, 5).reshape(FT, P, GB, P))

    ffn(0, 0)
    pw = A(pool_w)[0].reshape(2, 2, 2, P, 2, P)
    parts.append(pw.transpose(0, 3, 1, 4, 2, 5).reshape(2, P, GB, P))
    ffn(0, 1)
    ffn(1, 0)
    g = rows_as_groups(A(conv_w_in)[0])
    parts.append(np.stack([g[8:16], g[16:24], g[0:8]], 1).reshape(24, P, GB, P))
    parts.append(rows_as_groups(A(conv_w_out)[0]))
    ffn(1, 1)
    g = rows_as_groups(A(w_in_2)[0])
    parts.append(g[12:16])
    parts.append(g[0:8])
    gates = np.zeros((1, P, GB, P), np.float32)
    for b in range(8):
        for part, w in enumerate((rg_w_a_2, rg_w_x_2)):
            r = slice(64 * (b % 2), 64 * (b % 2) + 64)
            gates[0, r, 2 * (b // 2) + part, r] = A(w)[0, b]
    parts.append(gates)
    parts.append(g[16:20])
    v = A(w_in_2)[0][:, 1024:1536].reshape(4, 2, P, 4, P)
    parts.append(v.transpose(0, 2, 1, 3, 4).reshape(4, P, GB, P))
    parts.append(rows_as_groups(A(w_out_2)[0]))
    parts.append(rows_as_groups(A(peer_w_query_2)[0].reshape(D, HP * P)))
    u = A(peer_u_2)[0].reshape(NK, NK, KT, P).transpose(1, 3, 2, 0)
    v = A(peer_v_2)[0].reshape(NK, NB, MB, KT, P).transpose(1, 3, 0, 2, 4).reshape(NB, KT, P, GB, P)
    parts.append(u)
    parts.append(v.reshape(NK, P, GB, P))
    sub_keys = np.ascontiguousarray(A(peer_sub_keys_2)[0].reshape(HP, NK, P).transpose(2, 0, 1))
    stream = np.concatenate(parts)
    ada = A(ada_w).reshape(2 * KT, P, 9 * D)
    smalls = np.concatenate([columns(A(c)), columns(A(ada_b)), columns(A(norm_g)), columns(A(pool_scale)), columns(A(conv_w)),
                             columns(A(final_g)), np.zeros((P, KT), np.float32), np.full((P, 1), 1e-6, np.float32)], 1)
    corr = np.concatenate([w / np.arange(1, w) for w in (2, 4, 8, 16)] + [np.zeros(6)])
    consts = np.concatenate([np.full((P, P), 1 / D), np.tile(corr, (P, 1))], 1).astype(np.float32)
    xin = np.ascontiguousarray(A(x)[0].T.reshape(KT, P, T).transpose(1, 0, 2))
    twice = lambda g: np.tile(A(g).reshape(64, 1), (2, 1))
    smalls2 = np.concatenate([columns(A(norm_mix_2)), twice(q_norm_2), twice(k_norm_2), columns(A(conv_w_2)), columns(A(conv_b_2)),
                              columns(A(rg_b_a_2)), columns(A(rg_b_x_2)), columns(A(rg_lambda_2)),
                              columns(A(out_norm_sb_2)), columns(A(out_norm_rg_2)), columns(A(norm_ffn_2)),
                              np.zeros((P, KT), np.float32), np.full((P, 1), 1e-6, np.float32)], 1)
    r = np.arange(P)
    key, query = r[:, None], r[None, :]
    consts2 = np.stack([(key // 64 == query // 64) / 64.0, key < query, np.full((P, P), 1 / 512), key == query, np.tile(r, (P, 1)),
                        -1.0 * (key >= query), -np.ones((P, P)), key == query, np.where(key < query, 0.0, -1e30)], 1).astype(np.float32)
    return {"stream": stream, "ada": ada, "smalls": smalls, "consts": consts, "smalls2": smalls2, "consts2": consts2,
            "keys": sub_keys, "xin": xin}


def kernel(**inputs):
    import concourse.bacc as bacc
    from concourse.bass_utils import run_bass_kernel_spmd

    nc = bacc.Bacc("TRN2", target_bir_lowering=False, num_devices=1)
    arrays, args = {}, []
    for name, a in layout(**inputs).items():
        arrays[name + "_dram"] = a
        args.append(nc.dram_tensor(name + "_dram", a.shape, mybir.dt.from_np(a.dtype), kind="ExternalInput").ap())
    args.append(nc.dram_tensor("out_dram", (P, KT, T), F32, kind="ExternalOutput").ap())
    build(nc, *args)
    r = run_bass_kernel_spmd(nc, [arrays], core_ids=[0])
    y = r.results[0]["out_dram"]
    return np.ascontiguousarray(y.transpose(2, 1, 0).reshape(1, T, D))
```

```python
import concourse.bass as bass
from concourse import mybir
import numpy as np

F32 = mybir.dt.float32
F32R = mybir.dt.float32r
BF16 = mybir.dt.bfloat16
U32 = mybir.dt.uint32
ALU = mybir.AluOpType
ACT = mybir.ActivationFunctionType
AXX = mybir.AxisListType.X

P = 128
T = 512
D = 1024
KT = D // P
FF = 2816
FT = FF // P
GB = 8
R = 4
LOOK = 3

SEG = {}
_at = 0
for _name, _n in (("ffn0_in", 2 * FT), ("ffn0_out", FT), ("pool", 2),
                  ("ffn1_in", 2 * FT), ("ffn1_out", FT),
                  ("ffn2_in", 2 * FT), ("ffn2_out", FT),
                  ("conv_in", 24), ("conv_out", 8),
                  ("ffn3_in", 2 * FT), ("ffn3_out", FT),
                  ("xr", 4), ("qk", 8), ("gates", 1), ("gr", 4), ("v", 4), ("mix_out", 8),
                  ("query", 16), ("up", 128), ("down", 128)):
    SEG[_name] = (_at, _n)
    _at += _n
NORM_TILES = (8, 8, 8, 8, 8, 8, 8, 8, 4, 4, 8)
ALL_NORMS = tuple(range(11))
SPLIT_NORMS = (0, 2, 3, 4, 5, 7, 8, 9, 10)
SCALED_NORMS = (0, 1) + SPLIT_NORMS[1:]
DECAY_STEPS = 18
CORR = {2: 0, 4: 1, 8: 4, 16: 11}
N_GROUPS = _at

SMALL = {}
_at = 0
for _name, _n in (("c", KT), ("ada_b", 18 * KT), ("norm_g", 6 * KT), ("pool_scale", KT),
                  ("conv_w", 3 * KT), ("final_g", KT), ("zero", KT), ("eps", 1)):
    SMALL[_name] = _at
    _at += _n
N_SMALL = _at

SMALL2 = {}
_at = 0
for _name, _n in (("norm_mix", KT), ("q_gain", 1), ("k_gain", 1), ("conv_w2", 16), ("conv_b2", 4),
                  ("b_a", 4), ("b_x", 4), ("lam", 4), ("out_gain", KT), ("norm_ffn", KT),
                  ("zero2", KT), ("eps2", 1)):
    SMALL2[_name] = _at
    _at += _n
N_SMALL2 = _at

HEADS = 8
QK_BANK = (4, 5, 2, 3)
CT = 4
N_PLAIN = 5
BLK, MASK, MEAN_H, IDENT, IOTA = range(N_PLAIN)
TRI, ONES, IDENT_R, FAR = range(4)
ATT_OFF = [0, 512, 896, 1152]
ATT_COLS = 1280
PH = 8
HP = 2 * PH
NK = 128
TOP = 16
TT = T // P
TC = 8
MB = 8
NB = NK // MB
LEAD = 8
CHUNKS = P // TC
GAP = 8
assert TT * (LEAD + CHUNKS + GAP) == NK and LEAD % 4 == GAP % 4 == CHUNKS % 4 == 0
LOWEST = -3.0e38
EARLY = NK // 2
UNITS = [(h, i) for h in range(HEADS) for i in reversed(range(CT))]


def at(c, i, m):
    return c if i is None else i * m + c


def tiles_before(norms, n):
    return sum(NORM_TILES[m] for m in norms if m < n)


def v_group(b, d):
    return SEG["down"][0] + MB * b + d


def build(nc, stream, ada, smalls, consts, smalls2, consts2, keys, xin, out):
    KB = 1024

    def place(name, kib, shape, dt):
        return nc.alloc_sbuf_tensor_at(name, shape, dt, offset=base + int(kib * KB))

    base = (nc.sbuf_base + 63) // 64 * 64
    raw = place("raw", 0, [P, R, GB, P], F32)
    whi = place("whi", 16, [P, R, GB, P], F32R)
    wlo = place("wlo", 32, [P, R, GB, P], F32R)
    x = place("x", 48, [P, KT, T], F32)
    hhi = place("hhi", 64, [P, KT, T], F32R)
    hlo = place("hlo", 80, [P, KT, T], F32R)
    small = place("small", 96, [P, N_SMALL], F32)
    mod = place("mod", 97.25, [P, 18 * KT], F32)
    coef = place("coef", 97.875, [P, 2, 6 * KT], F32)
    cond = place("cond", 98.5, [P, KT], F32)
    one_col = place("one_col", 98.625, [P, 1], F32)
    corr = place("corr", 98.75, [P, 32], F32)
    mean_d = place("mean_d", 99, [P, P], F32)
    uhi = place("uhi", 99.5, [P, FT, T], F32R)
    ulo = place("ulo", 143.5, [P, FT, T], F32R)
    silu = place("silu", 187.5, [P, 2, T], F32)
    u32 = place("u32", 191.5, [P, 2, T], F32)
    ada_raw = place("ada_raw", 195.5, [P, 4, T], F32)
    ada_accs = [place(f"ada_acc{h}", 203.5 + 2 * h, [P, T], F32) for h in range(2)]
    first_raw = place("first_raw", 123.5, [P, KT, 4 * T], F32)
    first_acc = place("first_acc", 187.5, [P, 4 * T], F32)
    sq = place("sq", 99.5, [P, 2, T], F32)
    sqsum = place("sqsum", 103.5, [P, T], F32)
    std = place("std", 101.5, [P, T], F32)
    rstd = place("rstd", 105.5, [P, T], F32)
    xn = place("xn", 107.5, [P, 2, T], F32)
    h32 = place("h32", 107.5, [P, KT, T], F32)
    pad0 = place("pad0", 120, [P, 2, 16 + T], F32)
    pad1 = place("pad1", 125, [P, 16 + T], F32)
    pad2 = place("pad2", 128, [P, 16 + T], F32)
    mix32 = place("mix32", 131, [P, 2, T], F32)
    yhi = place("yhi", 136, [P, KT, T], F32R)
    ylo = place("ylo", 152, [P, KT, T], F32R)
    cgate = place("cgate", 168, [P, 2, T], F32)
    cu = place("cu", 172, [P, 2, 2 + T], F32)
    cv = place("cv", 177, [P, 2, T], F32)
    y32 = place("y32", 181, [P, 2, T], F32)

    q_hi = place("q_hi", 100, [P, CT, T], F32R)
    q_lo = place("q_lo", 108, [P, CT, T], F32R)
    k_hi = place("k_hi", 116, [P, CT, T], F32R)
    k_lo = place("k_lo", 124, [P, CT, T], F32R)
    v_hi = place("v_hi", 132, [P, CT, T], F32R)
    v_lo = place("v_lo", 140, [P, CT, T], F32R)
    o = place("o", 148, [P, KT, T], F32)
    xpad = place("xpad", 164, [P, 2, 8 + T], F32)
    qsq = place("qsq", 168.25, [P, 2, T], F32)
    xc = place("xc", 172.25, [P, CT, T], F32)
    xc_hi = place("xc_hi", 148, [P, CT, T], F32R)
    xc_lo = place("xc_lo", 156, [P, CT, T], F32R)
    qstd = place("qstd", 184.25, [P, T], F32)
    qrstd = place("qrstd", 186.25, [P, T], F32)
    r_gate = place("r_gate", 188.25, [P, CT, T], F32)
    i_gate = place("i_gate", 140, [P, CT, T], F32)
    a_dec = place("a_dec", 148, [P, CT, T], F32)
    tanh_a = place("tanh_a", 156, [P, CT, T], F32)
    qn = place("qn", 132, [P, 2, T], F32)
    cx = place("cx", 136, [P, 2, T], F32)
    sp = place("sp", 164, [P, 2, T], F32)
    l_hi = place("l_hi", 168, [P, 2, ATT_COLS], F32R)
    l_lo = place("l_lo", 178, [P, 2, ATT_COLS], F32R)
    w32 = place("w32", 188, [P, 2, T], F32)
    w_hi = place("w_hi", 192, [P, 2, T], F32R)
    w_lo = place("w_lo", 196, [P, 2, T], F32R)
    round_raw = place("round_raw", 195.5, [P, 4 * P], F32)
    small2 = place("small2", 202.5, [P, N_SMALL2], F32)
    decay = place("decay", 203, [P, 8, CT], F32)
    sq_plain = place("sq_plain", 203.25, [P, N_PLAIN, P], F32)
    sq_round = place("sq_round", 205.75, [P, 4, P], F32R)

    key_hi = place("key_hi", 124, [P, HP, NK], F32R)
    key_lo = place("key_lo", 132, [P, HP, NK], F32R)
    key32 = place("key32", 140, [P, HP, NK], F32)
    qt_hi = place("qt_hi", 148, [P, 2, T], F32R)
    qt_lo = place("qt_lo", 152, [P, 2, T], F32R)
    top_v = place("top_v", 156, [P, PH, 2, TT, TOP], F32)
    top_i = place("top_i", 160, [P, PH, 2, TT, TOP], U32)
    top_b = place("top_b", 172, [P, PH, 2, TT, TOP], BF16)
    rest1 = place("rest1", 178, [P, TT, NK], F32)
    cand = place("cand", 122, [P, PH, TOP * TOP], F32)
    rest2 = place("rest2", 130, [P, PH, TOP * TOP], F32)
    is_pos = place("is_pos", 138, [P, PH, TOP, TOP], BF16)
    prod = place("prod", 142, [P, PH, TOP, TOP], BF16)
    best_v = place("best_v", 190, [P, PH, TOP], F32)
    best_p = place("best_p", 190.5, [P, PH, TOP], U32)
    pos_u = place("pos_u", 191, [P, 2, PH, TOP], U32)
    pos_b = place("pos_b", 192, [P, 2, PH, TOP], BF16)
    below = place("below", 192.5, [P, PH, TOP], F32)
    expo = place("expo", 193, [P, PH, TOP], F32)
    esum = place("esum", 193.5, [P, 2, PH], F32)
    chosen = place("chosen", 194, [P, 3, PH * TOP], F32)
    left = place("left", 195.5, [P, 2, P], F32)
    iota_b = place("iota_b", 202, [P, P], BF16)
    hot_n = place("hot_n", 177, [P, 2, TC, P], BF16)
    hot_m = place("hot_m", 181, [P, 2, TC, P], BF16)
    hot_w = place("hot_w", 185, [P, 2, 3, TC, P], BF16)
    pick = place("pick", 197, [P, 5, T], BF16)
    spread = place("spread", 100, [P, NK, P], F32)
    g_ring = place("g_ring", 172, [P, 4, T], F32)
    act_out = place("act_out", 164, [P, 4, T], F32)
    act_in = place("act_in", 185, [P, 4, T], F32)
    we32 = place("we32", 181, [P, 2, T], F32)
    we = place("we", 100, [P, 2, 2, MB, T], F32R)

    expert_weights = nc.dram_tensor("expert_weights", (TT, P, NK, P), F32).ap()
    expert_acts = nc.dram_tensor("expert_acts", (NK, P, T), F32).ap()

    psum = [nc.alloc_psum_tensor(f"bank{b}", [P, T], F32) for b in range(8)]

    sems = {}

    def sem(name):
        if name not in sems:
            sems[name] = nc.alloc_semaphore(name)
        return sems[name]

    const_landed = sem("const_landed")
    raw_landed = [sem(f"raw_landed{s}") for s in range(R)]
    hi_ready = sem("hi_ready")
    lo_ready = sem("lo_ready")
    pe_groups = sem("pe_groups")
    x_ready = sem("x_ready")
    sq_ready = sem("sq_ready")
    sq_used = sem("sq_used")
    ms_ready = sem("ms_ready")
    std_ready = sem("std_ready")
    rstd_ready = sem("rstd_ready")
    xn_ready = sem("xn_ready")
    hhi_ready = sem("hhi_ready")
    h_ready = sem("h_ready")
    silu_ready = sem("silu_ready")
    u_mul = sem("u_mul")
    uhi_ready = sem("uhi_ready")
    u_ready = sem("u_ready")
    cond_ready = sem("cond_ready")
    setup_done = sem("setup_done")
    ada_landed = [sem(f"ada_landed{s}") for s in range(4)]
    first_landed = [sem(f"first_landed{k}") for k in range(KT)]
    ada_used = sem("ada_used")
    ada_summed = sem("ada_summed")
    mod_ready = sem("mod_ready")
    coef_ready = sem("coef_ready")
    gate_ready = sem("gate_ready")
    bank_done = sem("bank_done")
    pool_h = sem("pool_h")
    pool_step = sem("pool_step")
    pool_mixed = sem("pool_mixed")
    pool_hi = sem("pool_hi")
    pool_ready = sem("pool_ready")
    cgate_ready = sem("cgate_ready")
    cu_ready = sem("cu_ready")
    cv_step = sem("cv_step")
    y32_ready = sem("y32_ready")
    yhi_ready = sem("yhi_ready")
    y_ready = sem("y_ready")
    out_done = sem("out_done")
    const2_landed = sem("const2_landed")
    const2_ready = sem("const2_ready")
    decay_step = sem("decay_step")
    decay_exp = sem("decay_exp")
    xpad_ready = sem("xpad_ready")
    conv2_step = sem("conv2_step")
    xc_ready = sem("xc_ready")
    xc_hi_ready = sem("xc_hi_ready")
    xc_lo_ready = sem("xc_lo_ready")
    qsq_ready = sem("qsq_ready")
    qms_ready = sem("qms_ready")
    qstd_ready = sem("qstd_ready")
    qrstd_ready = sem("qrstd_ready")
    qn_ready = sem("qn_ready")
    qhi_ready = sem("qhi_ready")
    q_ready = sem("q_ready")
    gate_products = sem("gate_products")
    gates_ready = sem("gates_ready")
    tanh_ready = sem("tanh_ready")
    a_ready = sem("a_ready")
    rg_step = sem("rg_step")
    rg_neg = sem("rg_neg")
    rg_root = sem("rg_root")
    gelu_ready = sem("gelu_ready")
    rg_done = sem("rg_done")
    vhi_ready = sem("vhi_ready")
    v_ready = sem("v_ready")
    z_ready = sem("z_ready")
    lnx_step = sem("lnx_step")
    sp_ready = sem("sp_ready")
    lhi_ready = sem("lhi_ready")
    l_ready = sem("l_ready")
    expo_ready = sem("expo_ready")
    w32_ready = sem("w32_ready")
    whi_ready = sem("whi_ready")
    w_ready = sem("w_ready")
    pv_done = sem("pv_done")
    o_ready = sem("o_ready")
    rg_out = sem("rg_out")
    keys_landed = sem("keys_landed")
    keys_hi = sem("keys_hi")
    keys_ready = sem("keys_ready")
    qthi_ready = sem("qthi_ready")
    qt_ready = sem("qt_ready")
    scores_done = sem("scores_done")
    top_step = sem("top_step")
    sel_step = sem("sel_step")
    below_ready = sem("below_ready")
    exp_ready = sem("exp_ready")
    chosen_ready = sem("chosen_ready")
    turned = sem("turned")
    pick_step = sem("pick_step")
    iota_ready = sem("iota_ready")
    hot_mark = sem("hot_mark")
    hot_ready = sem("hot_ready")
    hot_third = sem("hot_third")
    hot_used = sem("hot_used")
    spread_ready = sem("spread_ready")
    spilled = sem("spilled")
    spilled_late = sem("spilled_late")
    acts_stored = [sem(f"acts_stored{s}") for s in range(4)]
    a_landed = [sem(f"a_landed{s}") for s in range(4)]
    g_landed = [sem(f"g_landed{s}") for s in range(4)]
    gelu_done = sem("gelu_done")
    we_mul = sem("we_mul")
    we_hi_ready = sem("we_hi_ready")
    we_ready = sem("we_ready")
    y_added = sem("y_added")

    def S(name, k=0, n=1):
        return small[:, SMALL[name] + k:SMALL[name] + k + n]

    def S2(name, k=0, n=1):
        return small2[:, SMALL2[name] + k:SMALL2[name] + k + n]

    def shift_of(n, k):
        return mod[:, 3 * n * KT + k:3 * n * KT + k + 1] if n < 6 else S2("zero2", k)

    def scale_of(n, k):
        if n < 6:
            return coef[:, 0, n * KT + k:n * KT + k + 1]
        return S2("norm_mix", k) if n == 7 else S2("norm_ffn", k) if n == 10 else S2("out_gain", k + (4 if n == 9 else 0))

    def hot_column(part, c, i):
        cols = pick[:, part, TC * c:TC * c + TC] if i is None else pick[:, part, bass.ds(i * (4 * TC) + TC * c, TC)]
        return cols.unsqueeze(2).to_broadcast([P, TC, P])

    BODY = 4
    BODIES = FT // BODY
    ADA_AT = {0: 2, 1: 8, 2: 13}
    LATE = 7
    assert FT == BODY * BODIES + 2 and ADA_AT[0] + BODIES == LATE and ADA_AT[1] + BODIES == ADA_AT[2] and ADA_AT[2] + BODIES == 18
    SUB_NORM = {0: 0, 1: 2, 2: 3, 3: 5}
    n_groups = N_GROUPS

    with nc.Block() as block:

        @block.sync
        def _(sp):
            sp.dma_start(small[:, :], smalls).then_inc(const_landed, 16)
            sp.dma_start(mean_d[:, :], consts[:, 0:P]).then_inc(const_landed, 16)
            sp.dma_start(corr[:, :], consts[:, P:P + 32]).then_inc(const_landed, 16)
            sp.dma_start(x[:, :, :], xin).then_inc(const_landed, 16)

            def load(c, i, m):
                s = c % R
                if c >= R:
                    sp.wait_ge(lo_ready, at(c - R + 1, i, m))
                sp.dma_start(raw[:, s, :, :], stream[at(c, i, m)] if i is None else stream[bass.ds(i * m + c, 1)].rearrange("a p g n -> (a p) g n")).then_inc(raw_landed[s], 16)

            for c in range(R):
                load(c, None, 0)
            n = (n_groups - R) // R
            with sp.Fori(0, n) as i:
                for j in range(R):
                    load(R + j, i, R)
            for c in range(R + n * R, n_groups):
                load(c, None, 0)
            sp.wait_ge(y_added, NB * KT)
            sp.dma_start(out, x[:, :, :]).then_inc(out_done, 16)
            sp.wait_ge(out_done, 16)

        @block.gpsimd
        def _(pool):
            def lo(c, i, m):
                s = c % R
                pool.wait_ge(hi_ready, at(c + 1, i, m))
                pool.tensor_tensor(wlo[:, s, :, :], raw[:, s, :, :], whi[:, s, :, :].bitcast(F32),
                                   ALU.subtract).then_inc(lo_ready, 1)

            def lo_range(first, last):
                n = (last - first) // R
                with pool.Fori(0, n) as i:
                    for j in range(first, first + R):
                        lo(j, i, R)
                for c in range(first + n * R, last):
                    lo(c, None, 0)

            up = SEG["up"][0]
            lo_range(0, up + LOOK)

            def third_rows(c, i):
                pool.wait_ge(hot_mark, at(c + 1, i, 4))
                if c >= 2:
                    pool.wait_ge(hot_used, at(c - 1, i, 4))
                pool.tensor_tensor(hot_w[:, c % 2, 2, :, :], hot_m[:, c % 2, :, :], hot_column(4, c, i), ALU.mult).then_inc(hot_third, 1)

            def columns_run(m0, n):
                with pool.Fori(0, n // 4) as i:
                    for m in range(m0, m0 + 4):
                        lo(up + m + LOOK, i, 4)

            columns_run(0, TT * LEAD)
            for tt in range(TT):
                m0 = TT * LEAD + tt * (CHUNKS + GAP)
                c0 = tt * CHUNKS
                if tt == 0:
                    for k in range(4):
                        third_rows(c0 + k, None)
                        lo(up + m0 + k + LOOK, None, 0)
                    m0, c0 = m0 + 4, c0 + 4
                with pool.Fori(0, CHUNKS // 4 - (tt == 0)) as i:
                    for k in range(4):
                        third_rows(c0 + k, i)
                        lo(up + m0 + k + LOOK, i, 4)
                columns_run(TT * LEAD + tt * (CHUNKS + GAP) + CHUNKS, GAP)
            lo_range(up + NK + LOOK, n_groups)

        @block.scalar
        def _(act):
            def hi(c, i=None, m=0):
                if c >= n_groups:
                    return
                s = c % R
                act.wait_ge(raw_landed[s], at(16 * (c // R + 1), i, 16 * m // R))
                if c >= R:
                    act.wait_ge(pe_groups, at(c - R + 1, i, m))
                act.activation(whi[:, s, :, :], raw[:, s, :, :], ACT.Copy).then_inc(hi_ready, 1)

            def ada_load(c, i=None, m=0):
                s = c % 4
                if c >= 4:
                    act.wait_ge(ada_used, at(c - 3, i, m))
                it, hf, k = c // 16, c // 8 % 2, c % 8
                if i is None:
                    src = ada[(it // 9) * KT + k, :, ((it % 9) * 2 + hf) * T:((it % 9) * 2 + hf + 1) * T]
                else:
                    src = ada[(it // 9) * KT + k, :, bass.ds(i * (2 * T) + ((it % 9) * 2 + hf) * T, T)]
                act.dma_start(ada_raw[:, s, :], src).then_inc(ada_landed[s], 16)

            def square(n, k, src=x, t0=0):
                s0 = tiles_before(ALL_NORMS, n)
                if n == 0 and k == 0:
                    act.wait_ge(const_landed, 64)
                elif 0 < n < 8 or n == 10:
                    act.wait_ge(x_ready, KT * (min(n, 8) - 1) + k + 1)
                if s0 + k >= 2:
                    act.wait_ge(sq_used, s0 + k - 1)
                act.activation(sq[:, k % 2, :], src[:, t0 + k, :], ACT.Square).then_inc(sq_ready, 1)

            def norm(n, h_out, src=x, t0=0, squared=0):
                for k in range(squared, NORM_TILES[n]):
                    square(n, k, src, t0)
                act.wait_ge(ms_ready, n + 1)
                act.activation(std[:, :], psum[7][:, :], ACT.Sqrt, bias=S("eps") if n < 7 else S2("eps2")).then_inc(std_ready, 1)
                if h_out is not None:
                    for k in range(NORM_TILES[n]):
                        act.wait_ge(xn_ready, tiles_before(SCALED_NORMS, n) + k + 1)
                        h_out(n, k)

            def h_high(n, k):
                o_k = k + (4 if n == 9 else 0)
                act.activation(hhi[:, o_k, :], h32[:, o_k, :], ACT.Identity, bias=shift_of(n, k)).then_inc(hhi_ready, 1)

            def ffn(q):
                g0 = SEG[f"ffn{q}_in"][0]
                it0 = ADA_AT.get(q)

                def tile(j, i, units=False):
                    g = g0 + 2 * j
                    t = FT * q + j
                    hi(g + LOOK, i, 2 * BODY)
                    hi(g + LOOK + 1, i, 2 * BODY)
                    act.wait_ge(pe_groups, at(g + 1, i, 2 * BODY))
                    if t >= 2:
                        act.wait_ge(u_mul, at(t - 1, i, BODY))
                    act.activation(silu[:, j % 2, :], psum[2 * (j % 2)][:, :], ACT.Silu).then_inc(silu_ready, 1)
                    act.wait_ge(u_mul, at(t + 1, i, BODY))
                    act.activation(uhi[:, j, :] if i is None else uhi[:, bass.ds(i * BODY + j, 1), :].rearrange("p a t -> p (a t)"), u32[:, j % 2, :], ACT.Copy).then_inc(uhi_ready, 1)
                    if units:
                        for k in range(4):
                            ada_load(16 * it0 + 4 * j + k, i, 16)

                for j in range(BODY):
                    tile(j, None, it0 is not None)
                with act.Fori(0, BODIES - 1) as i:
                    for j in range(BODY, 2 * BODY):
                        tile(j, i, it0 is not None)
                for j in range(BODY * BODIES, FT):
                    tile(j, None)
                g1 = SEG[f"ffn{q}_out"][0]
                for half in range(2):
                    c = g1 + half * (FT // 2) + LOOK
                    hi(c)
                    if q == 0:
                        for k in range(8):
                            ada_load(16 * LATE + 8 * half + k)
                    with act.Fori(0, 2) as i:
                        for j in range(4):
                            hi(c + 1 + j, i, 4)
                    hi(c + 9)
                    hi(c + 10)

            act.wait_ge(const_landed, 64)
            act.activation(cond[:, :], S("c", 0, KT), ACT.Silu).then_inc(cond_ready, 1)
            for k in range(KT):
                act.dma_start(first_raw[:, k, :], ada[k, :, 0:4 * T]).then_inc(first_landed[k], 16)
            for k in range(KT):
                square(0, k)
            for c in range(LOOK):
                hi(c)
            norm(0, h_high, squared=KT)
            ffn(0)
            def pool_out(n, k):
                if k == 0:
                    act.wait_ge(coef_ready, 2)
                if k >= 2:
                    act.wait_ge(pool_mixed, k - 1)
                act.activation(pad0[:, k % 2, 16:16 + T], xn[:, k % 2, :], ACT.Identity, bias=shift_of(n, k), scale=scale_of(n, k)).then_inc(pool_h, 1)
                if k >= 1:
                    pool_round(k - 1)

            def pool_round(k):
                act.wait_ge(pool_mixed, k + 1)
                act.activation(hhi[:, k, :], mix32[:, k % 2, :], ACT.Copy).then_inc(pool_hi, 1)

            norm(1, pool_out)
            pool_round(KT - 1)
            hi(SEG["pool"][0] + LOOK)
            hi(SEG["pool"][0] + LOOK + 1)
            norm(2, h_high)
            ffn(1)
            norm(3, h_high)
            ffn(2)
            norm(4, h_high)
            g0 = SEG["conv_in"][0]

            def conv_tile(j, i):
                g = g0 + 3 * j
                hi(g + LOOK, i, 12)
                act.wait_ge(pe_groups, at(g + 1, i, 12))
                if j >= 2:
                    act.wait_ge(cu_ready, at(j - 1, i, 4))
                act.activation(cgate[:, j % 2, :], psum[3 * (j % 2)][:, :], ACT.Copy).then_inc(cgate_ready, 1)
                hi(g + LOOK + 1, i, 12)
                hi(g + LOOK + 2, i, 12)
                act.wait_ge(y32_ready, at(j + 1, i, 4))
                act.activation(yhi[:, j, :], y32[:, j % 2, :], ACT.Copy).then_inc(yhi_ready, 1)

            for j in range(KT):
                conv_tile(j, None)
            g0 = SEG["conv_out"][0]
            for c in range(KT):
                hi(g0 + c + LOOK)
                if c >= 2:
                    square(5, c - 2)
            norm(5, h_high, squared=KT - 2)
            act.wait_ge(mod_ready, 18)
            act.dma_start(small2[:, :], smalls2).then_inc(const2_landed, 16)
            act.dma_start(sq_plain[:, :, :], consts2[:, 0:N_PLAIN, :]).then_inc(const2_landed, 16)
            act.dma_start(round_raw[:, :], consts2[:, N_PLAIN:, :].rearrange("p a n -> p (a n)")).then_inc(const2_landed, 16)
            act.wait_ge(const2_landed, 48)
            act.activation(sq_round[:, :, :].rearrange("p a n -> p (a n)"), round_raw[:, :], ACT.Copy).then_inc(const2_ready, 1)
            act.wait_ge(decay_step, 1)
            act.activation(decay[:, 1, :], decay[:, 0, :], ACT.Exp, scale=-1.0).then_inc(decay_exp, 1)
            ffn(3)
            norm(6, None)
            norm(7, h_high)
            g0 = SEG["xr"][0]

            def round_xc(c):
                act.wait_ge(xc_ready, c + 1)
                act.activation(xc_hi[:, c, :], xc[:, c, :], ACT.Copy).then_inc(xc_hi_ready, 1)

            act.wait_ge(setup_done, 3)
            for c in range(CT):
                hi(g0 + c + LOOK)
                act.wait_ge(pe_groups, g0 + c + 1)
                if c >= 2:
                    act.wait_ge(xc_ready, c - 1)
                act.activation(xpad[:, c % 2, 8:8 + T], psum[c][:, :], ACT.Copy).then_inc(xpad_ready, 1)
                if c:
                    round_xc(c - 1)
            g0 = SEG["qk"][0]

            def q_std(t):
                act.wait_ge(qms_ready, t + 1)
                if t:
                    act.wait_ge(qrstd_ready, t)
                act.activation(qstd[:, :], psum[6 + t % 2][:, :], ACT.Sqrt, bias=S2("eps2")).then_inc(qstd_ready, 1)

            def q_round(t):
                act.wait_ge(qn_ready, t + 1)
                dst = q_hi if t < CT else k_hi
                act.activation(dst[:, t % CT, :], qn[:, t % 2, :], ACT.Copy).then_inc(qhi_ready, 1)

            for t in range(2 * CT):
                hi(g0 + t + LOOK)
                act.wait_ge(pe_groups, g0 + t + 1)
                if t >= 2:
                    act.wait_ge(qms_ready, t - 1)
                act.activation(qsq[:, t % 2, :], psum[QK_BANK[t % 4]][:, :], ACT.Square).then_inc(qsq_ready, 1)
                if t == 0:
                    round_xc(CT - 1)
                if t:
                    q_std(t - 1)
                if t >= 2:
                    q_round(t - 2)
            q_std(2 * CT - 1)
            q_round(2 * CT - 2)
            q_round(2 * CT - 1)
            hi(SEG["gates"][0] + LOOK)
            act.wait_ge(decay_step, DECAY_STEPS)
            for c in range(CT):
                if c < CT - 1:
                    act.wait_ge(gate_products, c + 1)
                else:
                    act.wait_ge(pe_groups, SEG["gates"][0] + 1)
                b = 2 * (c % 2)
                act.activation(r_gate[:, c, :], psum[b][:, :], ACT.Sigmoid, bias=S2("b_a", c)).then_inc(gates_ready, 1)
                act.activation(i_gate[:, c, :], psum[b + 1][:, :], ACT.Sigmoid, bias=S2("b_x", c)).then_inc(gates_ready, 1)
                act.wait_ge(gates_ready, 2 * c + 2)
                act.activation(tanh_a[:, c, :], r_gate[:, c, :], ACT.Tanh, scale=decay[:, 7, c:c + 1]).then_inc(tanh_ready, 1)
            for c in range(CT):
                act.activation(a_dec[:, c, :], r_gate[:, c, :], ACT.Exp, scale=decay[:, 7, c:c + 1]).then_inc(a_ready, 1)
            for c in range(CT):
                act.wait_ge(rg_neg, c + 1)
                act.activation(r_gate[:, c, :], tanh_a[:, c, :], ACT.Sqrt, scale=-1.0).then_inc(rg_root, 1)
            g0 = SEG["gr"][0]
            for c in range(CT):
                hi(g0 + c + LOOK)
                act.wait_ge(pe_groups, g0 + c + 1)
                act.wait_ge(rg_step, 3 * (c + 1))
                act.activation(xc[:, c, :], psum[4 + c][:, :], ACT.Gelu_apprx_tanh).then_inc(gelu_ready, 1)
            g0 = SEG["v"][0]
            for c in range(CT):
                hi(g0 + c + LOOK)
            act.wait_ge(pe_groups, g0 + CT)
            act.wait_ge(q_ready, 2 * CT)
            act.wait_ge(rg_done, CT)
            for c in range(CT):
                act.activation(v_hi[:, c, :], psum[c][:, :], ACT.Copy).then_inc(vhi_ready, 1)
            act.preload_act_table_set("natural_log_exp_and_others")
            steps = [0]

            def weights(u):
                h, i = UNITS[u]
                n = T - P * i
                act.wait_ge(expo_ready, u + 1)
                if u >= 2:
                    act.wait_ge(w_ready, u - 1)
                act.activation(w32[:, u % 2, 0:n], psum[u % 4][:, 0:n], ACT.Exp).then_inc(w32_ready, 1)

            for u, (h, i) in enumerate(UNITS):
                n = T - P * i
                act.wait_ge(z_ready, u + 1)
                if u >= 2:
                    act.wait_ge(l_ready, u - 1)
                for src, func, kw in ((psum[u % 4][:, 0:n], ACT.Abs, {}), (sp[:, u % 2, 0:n], ACT.Exp, {"scale": -1.0}),
                                      (sp[:, u % 2, 0:n], ACT.Ln, {"bias": one_col[:, :]})):
                    act.activation(sp[:, u % 2, 0:n], src, func, **kw).then_inc(lnx_step, 1)
                    steps[0] += 1
                    if func == ACT.Abs and u >= 2:
                        weights(u - 2)
                    if func != ACT.Ln:
                        act.wait_ge(lnx_step, steps[0])
            weights(len(UNITS) - 2)
            weights(len(UNITS) - 1)
            act.wait_ge(o_ready, HEADS)
            act.dma_start(key32[:, :, :], keys).then_inc(keys_landed, 16)
            for n, t0 in ((8, 0), (9, CT)):
                norm(n, h_high, o, t0)
            act.wait_ge(keys_landed, 16)
            act.activation(key_hi[:, :, :], key32[:, :, :], ACT.Copy).then_inc(keys_hi, 1)
            g0 = SEG["mix_out"][0]
            for c in range(KT):
                hi(g0 + c + LOOK)
                if c >= 2:
                    square(10, c - 2)
            norm(10, h_high, squared=KT - 2)
            g0 = SEG["query"][0]
            for t in range(HP):
                hi(g0 + t + LOOK)
                act.wait_ge(pe_groups, g0 + t + 1)
                if t >= 2:
                    act.wait_ge(scores_done, t - 1)
                act.activation(qt_hi[:, t % 2, :], psum[t % 2][:, :], ACT.Copy).then_inc(qthi_ready, 1)
            up = SEG["up"][0]

            def store_acts(m, i):
                act.wait_ge(gelu_done, at(m + 1, i, 4))
                dst = expert_acts[m] if i is None else expert_acts[bass.ds(i * 4 + m, 1)].rearrange("a n t -> (a n) t")
                act.dma_start(dst, act_out[:, m % 4, :]).then_inc(acts_stored[m % 4], 16)

            def column(m, i):
                hi(up + m + LOOK, i, 4)
                act.wait_ge(pe_groups, at(up + m + 1, i, 4))
                if m >= 4:
                    act.wait_ge(acts_stored[m % 4], at(16 * (m // 4), i, 16))
                act.activation(act_out[:, m % 4, :], psum[4 + m % 4][:, :], ACT.Gelu_apprx_tanh).then_inc(gelu_done, 1)
                if m:
                    store_acts(m - 1, i)

            def columns_run(m0, n):
                if m0 == 0:
                    for m in range(4):
                        column(m, None)
                    m0, n = 4, n - 4
                with act.Fori(0, n // 4) as i:
                    for m in range(m0, m0 + 4):
                        column(m, i)

            def take_rows(c, i, cols):
                act.wait_ge(hot_used, at(c + 1, i, 4))
                for half in range(2):
                    k = cols + 4 * half
                    dst = spread[:, :, bass.ds(i * (4 * TC) + k, 4)]
                    act.activation(dst.rearrange("p m t -> p t m"), psum[2 * (c % 2) + half][:, :].rearrange("p (t m) -> p t m", t=4), ACT.Copy).then_inc(spread_ready, 1)

            for tt in range(TT):
                columns_run(tt * LEAD, LEAD)
                act.wait_ge(below_ready, tt + 1)
                act.activation(expo[:, :, :], below[:, :, :], ACT.Exp).then_inc(exp_ready, 1)
            for tt in range(TT):
                m0 = TT * LEAD + tt * (CHUNKS + GAP)
                if tt:
                    act.wait_ge(spilled, 16 * tt)
                with act.Fori(0, CHUNKS // 4) as i:
                    for k in range(4):
                        column(m0 + k, i)
                        take_rows(CHUNKS * tt + k, i, TC * k)
                act.wait_ge(spread_ready, 2 * CHUNKS * (tt + 1))
                if tt < TT - 1:
                    act.dma_start(expert_weights[tt], spread[:, :, :]).then_inc(spilled, 16)
                else:
                    act.dma_start(expert_weights[tt][:, 0:EARLY, :], spread[:, 0:EARLY, :]).then_inc(spilled, 16)
                    act.dma_start(expert_weights[tt][:, EARLY:NK, :], spread[:, EARLY:NK, :]).then_inc(spilled_late, 16)
                if tt < TT - 1:
                    columns_run(m0 + CHUNKS, GAP)
            def load_column(m, i):
                s = m % 4
                if m >= 4:
                    act.wait_ge(we_mul, at(m - 3, i, 2 * MB))
                if i is None:
                    g, a = expert_weights[:, :, m, :].rearrange("a n t -> n a t"), expert_acts[m]
                else:
                    g = expert_weights[:, :, bass.ds(i * (2 * MB) + m, 1), :].rearrange("a n m t -> n a (m t)")
                    a = expert_acts[bass.ds(i * (2 * MB) + m, 1)].rearrange("a n t -> (a n) t")
                act.dma_start(g_ring[:, s, :].rearrange("p (a t) -> p a t", a=TT), g).then_inc(g_landed[s], 16)
                act.dma_start(act_in[:, s, :], a).then_inc(a_landed[s], 16)

            def out_step(b, i, js=range(MB)):
                for j in js:
                    m = MB * b + j
                    if b:
                        hi(v_group(b - 1, j) + LOOK, i, 2 * MB)
                    if b < NB:
                        if m + 3 < NK:
                            load_column(m + 3, i)
                        act.wait_ge(we_mul, at(m + 1, i, 2 * MB))
                        if b >= 2 and j == 0:
                            act.wait_ge(pe_groups, at(v_group(b - 2, KT - 1) + 1, i, 2 * MB))
                        act.activation(we[:, b % 2, 0, j, :], we32[:, m % 2, :], ACT.Copy).then_inc(we_hi_ready, 1)

            columns_run(NK - GAP, GAP // 2)
            act.wait_ge(spilled, 16 * TT)
            for k in range(4):
                act.wait_ge(acts_stored[k], 16 * 3)
            for m in range(3):
                load_column(m, None)
            for k in range(GAP // 2):
                column(NK - GAP // 2 + k, None)
                out_step(0, None, range(2 * k, 2 * k + 2))
            store_acts(NK - 1, None)
            act.wait_ge(spilled_late, 16)
            for k in range(4):
                act.wait_ge(acts_stored[k], 16 * NK // 4)
            out_step(1, None)
            with act.Fori(0, NB // 2 - 2) as i:
                out_step(2, i)
                out_step(3, i)
            for b in range(NB - 2, NB + 1):
                out_step(b, None)

        @block.vector
        def _(dve):
            def ada_units(c, n, i=None, m=0):
                acc = ada_accs[c // 8 % 2]
                for u in range(c, c + n):
                    k = u % 8
                    if k == 0 and c >= 16:
                        dve.wait_ge(ada_summed, at(c // 16, i, m // 16))
                    dve.wait_ge(ada_landed[u % 4], at(16 * (u // 4 + 1 - 8), i, 4 * m))
                    if k:
                        dve.wait_ge(ada_used, at(u, i, m))
                        dve.scalar_tensor_tensor(acc[:, :], ada_raw[:, u % 4, :], cond[:, k:k + 1], acc[:, :],
                                                 ALU.mult, ALU.add).then_inc(ada_used, 1)
                    else:
                        dve.tensor_scalar(acc[:, :], ada_raw[:, u % 4, :], cond[:, k:k + 1], None,
                                          ALU.mult).then_inc(ada_used, 1)

            def ada_finish(it, i=None, m=0):
                dve.wait_ge(ada_summed, at(it + 1, i, m))
                cols = mod[:, it * KT:(it + 1) * KT] if i is None else mod[:, bass.ds(i * KT + it * KT, KT)]
                bias = S("ada_b", it * KT, KT) if i is None else small[:, bass.ds(i * KT + (SMALL["ada_b"] + it * KT), KT)]
                dve.tensor_tensor(cols, psum[6][:, 0:KT], bias, ALU.add).then_inc(mod_ready, 1)

            def scales(n):
                dve.wait_ge(mod_ready, 3 * n + 2)
                dve.scalar_tensor_tensor(coef[:, 0, n * KT:(n + 1) * KT], mod[:, (3 * n + 1) * KT:(3 * n + 2) * KT], 1.0,
                                         S("norm_g", n * KT, KT), ALU.add, ALU.mult).then_inc(coef_ready, 1)
                dve.wait_ge(coef_ready, n + 1)

            def gates(n, factor):
                dve.wait_ge(mod_ready, 3 * n + 3)
                dst, gate = coef[:, 1, n * KT:(n + 1) * KT], mod[:, (3 * n + 2) * KT:(3 * n + 3) * KT]
                if isinstance(factor, float):
                    dve.tensor_scalar(dst, gate, factor, None, ALU.mult).then_inc(gate_ready, 1)
                else:
                    dve.tensor_tensor(dst, gate, factor, ALU.mult).then_inc(gate_ready, 1)
                dve.wait_ge(gate_ready, n + 1)

            def add_square(n, k):
                s0 = tiles_before(ALL_NORMS, n)
                dve.wait_ge(sq_ready, s0 + k + 1)
                if k:
                    dve.wait_ge(sq_used, s0 + k)
                    dve.tensor_tensor(sqsum[:, :], sqsum[:, :], sq[:, k % 2, :], ALU.add).then_inc(sq_used, 1)
                else:
                    dve.tensor_copy(sqsum[:, :], sq[:, 0, :]).then_inc(sq_used, 1)

            def inverse_root(n):
                dve.wait_ge(std_ready, n + 1)
                dve.reciprocal(rstd[:, :], std[:, :]).then_inc(rstd_ready, 1)
                dve.wait_ge(rstd_ready, n + 1)

            def norm_rest(n, src=x, t0=0):
                inverse_root(n)
                o_k = 4 if n == 9 else 0
                for k in range(NORM_TILES[n]):
                    dve.scalar_tensor_tensor(h32[:, k + o_k, :], src[:, t0 + k, :], scale_of(n, k), rstd[:, :], ALU.mult, ALU.mult).then_inc(xn_ready, 1)
                for k in range(NORM_TILES[n]):
                    dve.wait_ge(hhi_ready, tiles_before(SPLIT_NORMS, n) + k + 1)
                    dve.scalar_tensor_tensor(hlo[:, k + o_k, :], h32[:, k + o_k, :], shift_of(n, k), hhi[:, k + o_k, :].bitcast(F32),
                                             ALU.add, ALU.subtract).then_inc(h_ready, 1)

            def ffn(q):
                g0 = SEG[f"ffn{q}_in"][0]
                it0 = ADA_AT.get(q)
                n = SUB_NORM[q]

                def tile(j, i):
                    g = g0 + 2 * j
                    t = FT * q + j
                    dve.wait_ge(silu_ready, at(t + 1, i, BODY))
                    dve.wait_ge(pe_groups, at(g + 2, i, 2 * BODY))
                    if t >= 2:
                        dve.wait_ge(uhi_ready, at(t - 1, i, BODY))
                    dve.tensor_tensor(u32[:, j % 2, :], silu[:, j % 2, :], psum[2 * (j % 2) + 1][:, :],
                                      ALU.mult).then_inc(u_mul, 1)
                    dve.wait_ge(uhi_ready, at(t + 1, i, BODY))
                    if i is None:
                        a, b = uhi[:, j, :], ulo[:, j, :]
                    else:
                        a, b = (z[:, bass.ds(i * BODY + j, 1), :].rearrange("p a t -> p (a t)") for z in (uhi, ulo))
                    dve.tensor_tensor(b, u32[:, j % 2, :], a.bitcast(F32), ALU.subtract).then_inc(u_ready, 1)

                def body(j0, i):
                    for j in range(j0, j0 + BODY):
                        tile(j, i)
                        if it0 is not None:
                            if j == BODY:
                                ada_finish(it0, i, 1)
                            ada_units(16 * it0 + 4 * j, 4, i, 16)

                body(0, None)
                with dve.Fori(0, BODIES - 1) as i:
                    body(BODY, i)
                for j in range(BODY * BODIES, FT):
                    tile(j, None)
                    if it0 is not None and j == BODY * BODIES:
                        ada_finish(it0 + BODIES - 1)
                gates(n, 0.5)
                g1 = SEG[f"ffn{q}_out"][0]
                for half in range(2):
                    if q == 0:
                        ada_units(16 * LATE + 8 * half, 8)
                    if half:
                        for k in range(4):
                            add_square(n + 1, k)
                    for d in range(4):
                        k = half * 4 + d
                        if d < 3:
                            dve.wait_ge(bank_done, 3 * (2 * q + half) + d + 1)
                        else:
                            dve.wait_ge(pe_groups, g1 + (half + 1) * (FT // 2))
                        dve.scalar_tensor_tensor(x[:, k, :], psum[4 - 4 * half + d][:, :],
                                                 coef[:, 1, n * KT + k:n * KT + k + 1], x[:, k, :],
                                                 ALU.mult, ALU.add).then_inc(x_ready, 1)
                        if k > 4:
                            add_square(n + 1, k - 1)
                add_square(n + 1, KT - 1)

            dve.memset(one_col[:, :], 1.0).then_inc(setup_done, 1)
            dve.wait_ge(const_landed, 64)
            dve.wait_ge(cond_ready, 1)
            for k in range(KT):
                add_square(0, k)
            for k in range(KT):
                dve.wait_ge(first_landed[k], 16)
                if k:
                    dve.wait_ge(ada_used, 4 * k)
                    dve.scalar_tensor_tensor(first_acc[:, :], first_raw[:, k, :], cond[:, k:k + 1], first_acc[:, :],
                                             ALU.mult, ALU.add).then_inc(ada_used, 4)
                else:
                    dve.tensor_scalar(first_acc[:, :], first_raw[:, k, :], cond[:, k:k + 1], None, ALU.mult).then_inc(ada_used, 4)
            dve.wait_ge(ada_summed, 2)
            dve.tensor_tensor(mod[:, 0:2 * KT], psum[6][:, 0:2 * KT], S("ada_b", 0, 2 * KT), ALU.add).then_inc(mod_ready, 2)
            scales(0)
            norm_rest(0)
            ffn(0)
            ada_finish(LATE)
            dve.memset(pad0[:, :, 0:16], 0.0).then_inc(setup_done, 1)
            dve.wait_ge(setup_done, 2)
            scales(1)
            gates(1, S("pool_scale", 0, KT))
            step = [0]

            def chained(ins):
                step[0] += 1
                ins.then_inc(pool_step, 1)
                dve.wait_ge(pool_step, step[0])

            def pool_mix(k):
                dve.wait_ge(pool_h, k + 1)
                if k:
                    dve.wait_ge(pool_mixed, k)
                w = 2 << (k // 2)
                src = pad0[:, k % 2, :]
                bufs, b, sft = [pad1, pad2], 0, 1
                while sft < w:
                    lo = 2 * sft - 1
                    dst = bufs[b]
                    chained(dve.tensor_tensor(dst[:, lo:16 + T], src[:, lo:16 + T], src[:, lo - sft:16 + T - sft], ALU.add))
                    src, b, sft = dst[:, :], 1 - b, 2 * sft
                if k >= 2:
                    dve.wait_ge(pool_hi, k - 1)
                chained(dve.tensor_tensor(src[:, 16:16 + w - 1], src[:, 16:16 + w - 1], corr[:, CORR[w]:CORR[w] + w - 1], ALU.mult))
                dve.scalar_tensor_tensor(mix32[:, k % 2, :], src[:, 16:16 + T], 1.0 / w, pad0[:, k % 2, 16:16 + T],
                                         ALU.mult, ALU.subtract).then_inc(pool_mixed, 1)
                if k:
                    pool_low(k - 1)

            def pool_low(k):
                dve.wait_ge(pool_hi, k + 1)
                dve.wait_ge(pool_mixed, k + 1)
                dve.tensor_tensor(hlo[:, k, :], mix32[:, k % 2, :], hhi[:, k, :].bitcast(F32), ALU.subtract).then_inc(pool_ready, 1)

            inverse_root(1)
            for k in range(KT + 1):
                if k < KT:
                    if k >= 2:
                        dve.wait_ge(pool_h, k - 1)
                    dve.tensor_tensor(xn[:, k % 2, :], x[:, k, :], rstd[:, :], ALU.mult).then_inc(xn_ready, 1)
                if k:
                    pool_mix(k - 1)
            pool_low(KT - 1)
            for k in range(KT):
                if k in (0, 4):
                    dve.wait_ge(pe_groups, SEG["pool"][0] + k // 4 + 1)
                dve.scalar_tensor_tensor(x[:, k, :], psum[k][:, :], coef[:, 1, KT + k:KT + k + 1], x[:, k, :],
                                         ALU.mult, ALU.add).then_inc(x_ready, 1)
                if k:
                    add_square(2, k - 1)
            add_square(2, KT - 1)
            scales(2)
            norm_rest(2)
            ffn(1)
            scales(3)
            norm_rest(3)
            ffn(2)
            scales(4)
            norm_rest(4)
            dve.memset(cu[:, :, 0:2], 0.0).then_inc(cv_step, 1)
            gates(4, 1.0)
            g0 = SEG["conv_in"][0]
            cstep = [1]

            def cchained(ins):
                cstep[0] += 1
                ins.then_inc(cv_step, 1)
                dve.wait_ge(cv_step, cstep[0])

            dve.wait_ge(cv_step, 1)
            for j in range(KT):
                b = 3 * (j % 2)
                dve.wait_ge(cgate_ready, j + 1)
                dve.wait_ge(pe_groups, g0 + 3 * j + 2)
                dve.tensor_tensor(cu[:, j % 2, 2:2 + T], cgate[:, j % 2, :], psum[b + 1][:, :], ALU.mult).then_inc(cu_ready, 1)
                dve.wait_ge(cu_ready, j + 1)
                if j:
                    dve.wait_ge(y32_ready, j)
                cchained(dve.tensor_scalar(cv[:, 0, :], cu[:, j % 2, 2:2 + T], S("conv_w", 2 * KT + j), None, ALU.mult))
                cchained(dve.scalar_tensor_tensor(cv[:, 1, :], cu[:, j % 2, 1:1 + T], S("conv_w", KT + j), cv[:, 0, :], ALU.mult, ALU.add))
                cchained(dve.scalar_tensor_tensor(cv[:, 0, :], cu[:, j % 2, 0:T], S("conv_w", j), cv[:, 1, :], ALU.mult, ALU.add))
                dve.wait_ge(pe_groups, g0 + 3 * j + 3)
                dve.tensor_tensor(y32[:, j % 2, :], cv[:, 0, :], psum[b + 2][:, :], ALU.mult).then_inc(y32_ready, 1)
                dve.wait_ge(yhi_ready, j + 1)
                dve.tensor_tensor(ylo[:, j, :], y32[:, j % 2, :], yhi[:, j, :].bitcast(F32), ALU.subtract).then_inc(y_ready, 1)
            g0 = SEG["conv_out"][0]
            for k in range(KT):
                dve.wait_ge(pe_groups, g0 + k + 1)
                dve.scalar_tensor_tensor(x[:, k, :], psum[k][:, :], coef[:, 1, 4 * KT + k:4 * KT + k + 1], x[:, k, :],
                                         ALU.mult, ALU.add).then_inc(x_ready, 1)
                if k:
                    add_square(5, k - 1)
            add_square(5, KT - 1)
            scales(5)
            norm_rest(5)
            dve.wait_ge(const2_landed, 48)
            dstep = [0]

            def dchained(ins):
                dstep[0] += 1
                ins.then_inc(decay_step, 1)
                dve.wait_ge(decay_step, dstep[0])

            def dk(j):
                return decay[:, j, 0:CT]

            dchained(dve.scalar_tensor_tensor(dk(0), S2("lam", 0, CT), -1.0, S2("lam", 0, CT), ALU.mult, ALU.max))
            dve.wait_ge(decay_exp, 1)
            dchained(dve.tensor_scalar(dk(2), dk(1), 2.0, None, ALU.add))
            dchained(dve.reciprocal(dk(3), dk(2)))
            dchained(dve.tensor_tensor(dk(2), dk(1), dk(3), ALU.mult))
            dchained(dve.tensor_tensor(dk(3), dk(2), dk(2), ALU.mult))
            dchained(dve.tensor_scalar(dk(4), dk(3), 1.0 / 17, None, ALU.mult))
            for q in (15, 13, 11, 9, 7, 5, 3):
                dchained(dve.scalar_tensor_tensor(dk(4), dk(4), 1.0 / q, dk(3), ALU.add, ALU.mult))
            dchained(dve.scalar_tensor_tensor(dk(5), dk(4), 1.0, dk(2), ALU.add, ALU.mult))
            dchained(dve.tensor_scalar(dk(6), S2("lam", 0, CT), -1.0, 0.0, ALU.mult, ALU.max))
            dchained(dve.scalar_tensor_tensor(dk(4), dk(5), 2.0, dk(6), ALU.mult, ALU.add))
            dchained(dve.tensor_scalar(dk(7), dk(4), -8.0, None, ALU.mult))
            dchained(dve.tensor_scalar(dk(5)[:, 0:1], S2("q_gain"), 0.125, None, ALU.mult))
            assert dstep[0] == DECAY_STEPS
            ffn(3)
            inverse_root(6)
            for k in range(KT):
                dve.scalar_tensor_tensor(x[:, k, :], x[:, k, :], S("final_g", k), rstd[:, :],
                                         ALU.mult, ALU.mult).then_inc(x_ready, 1)
                if k:
                    add_square(7, k - 1)
            add_square(7, KT - 1)
            norm_rest(7)
            dve.memset(xpad[:, :, 0:8], 0.0).then_inc(setup_done, 1)
            xstep = [0]

            def xchained(ins):
                xstep[0] += 1
                ins.then_inc(conv2_step, 1)
                dve.wait_ge(conv2_step, xstep[0])

            dve.wait_ge(setup_done, 3)
            for c in range(CT):
                dve.wait_ge(xpad_ready, c + 1)
                row = xpad[:, c % 2, :]
                xchained(dve.tensor_scalar(cx[:, 0, :], row[:, 8:8 + T], S2("conv_w2", 3 * CT + c), S2("conv_b2", c), ALU.mult, ALU.add))
                xchained(dve.scalar_tensor_tensor(cx[:, 1, :], row[:, 7:7 + T], S2("conv_w2", 2 * CT + c), cx[:, 0, :], ALU.mult, ALU.add))
                xchained(dve.scalar_tensor_tensor(cx[:, 0, :], row[:, 6:6 + T], S2("conv_w2", CT + c), cx[:, 1, :], ALU.mult, ALU.add))
                dve.scalar_tensor_tensor(xc[:, c, :], row[:, 5:5 + T], S2("conv_w2", c), cx[:, 0, :], ALU.mult, ALU.add).then_inc(xc_ready, 1)
                dve.wait_ge(xc_ready, c + 1)
                dve.wait_ge(xc_hi_ready, c + 1)
                dve.tensor_tensor(xc_lo[:, c, :], xc[:, c, :], xc_hi[:, c, :].bitcast(F32), ALU.subtract).then_inc(xc_lo_ready, 1)

            def q_low(t):
                dve.wait_ge(qhi_ready, t + 1)
                a, b = (q_hi, q_lo) if t < CT else (k_hi, k_lo)
                dve.tensor_tensor(b[:, t % CT, :], qn[:, t % 2, :], a[:, t % CT, :].bitcast(F32), ALU.subtract).then_inc(q_ready, 1)

            for t in range(2 * CT):
                dve.wait_ge(qstd_ready, t + 1)
                if t:
                    dve.wait_ge(qn_ready, t)
                dve.reciprocal(qrstd[:, :], qstd[:, :]).then_inc(qrstd_ready, 1)
                dve.wait_ge(qrstd_ready, t + 1)
                if t >= 2:
                    dve.wait_ge(q_ready, t - 1)
                gain = dk(5)[:, 0:1] if t < CT else S2("k_gain")
                dve.scalar_tensor_tensor(qn[:, t % 2, :], psum[QK_BANK[t % 4]][:, :], gain, qrstd[:, :], ALU.mult, ALU.mult).then_inc(qn_ready, 1)
                if t:
                    q_low(t - 1)
            q_low(2 * CT - 1)
            for c in range(CT):
                dve.wait_ge(gates_ready, 2 * c + 2)
                dve.tensor_tensor(i_gate[:, c, :], i_gate[:, c, :], xc[:, c, :], ALU.mult).then_inc(rg_step, 1)
                dve.wait_ge(a_ready, c + 1)
                dve.tensor_tensor(r_gate[:, c, :], a_dec[:, c, :], a_dec[:, c, :], ALU.mult).then_inc(rg_step, 1)
                dve.wait_ge(rg_step, 3 * c + 2)
                dve.scalar_tensor_tensor(tanh_a[:, c, :], r_gate[:, c, :], 1.0, tanh_a[:, c, :], ALU.add, ALU.mult).then_inc(rg_neg, 1)
                dve.wait_ge(rg_root, c + 1)
                dve.tensor_tensor(i_gate[:, c, :], i_gate[:, c, :], r_gate[:, c, :], ALU.mult).then_inc(rg_step, 1)
                dve.wait_ge(rg_step, 3 * c + 3)
                dve.tensor_tensor_scan(o[:, CT + c, :], a_dec[:, c, :], i_gate[:, c, :], 0.0, ALU.mult, ALU.add).then_inc(rg_done, 1)
            for c in range(CT):
                dve.wait_ge(gelu_ready, c + 1)
                dve.wait_ge(rg_done, c + 1)
                dve.tensor_tensor(o[:, CT + c, :], o[:, CT + c, :], xc[:, c, :], ALU.mult).then_inc(rg_out, 1)
            for c in range(CT):
                dve.wait_ge(vhi_ready, c + 1)
                dve.tensor_tensor(v_lo[:, c, :], psum[c][:, :], v_hi[:, c, :].bitcast(F32), ALU.subtract).then_inc(v_ready, 1)
            lsteps = [0]

            def split_w(u):
                h, i = UNITS[u]
                n = T - P * i
                dve.wait_ge(w32_ready, u + 1)
                if u >= 2:
                    dve.wait_ge(pv_done, u - 1)
                dve.tensor_copy(w_hi[:, u % 2, 0:n], w32[:, u % 2, 0:n]).then_inc(whi_ready, 1)
                dve.wait_ge(whi_ready, u + 1)
                dve.tensor_tensor(w_lo[:, u % 2, 0:n], w32[:, u % 2, 0:n], w_hi[:, u % 2, 0:n].bitcast(F32), ALU.subtract).then_inc(w_ready, 1)
                if i == 0 and h:
                    take_o(h - 1)

            def take_o(h):
                dve.wait_ge(pv_done, CT * (h + 1))
                rows = slice(64 * (h % 2), 64 * (h % 2) + 64)
                dve.tensor_copy(o[rows, h // 2, :], psum[4 + h % 2][rows, :]).then_inc(o_ready, 1)

            for u, (h, i) in enumerate(UNITS):
                n = T - P * i
                buf, cols = sp[:, u % 2, 0:n], slice(ATT_OFF[i], ATT_OFF[i] + n)
                if u >= 2:
                    split_w(u - 2)
                dve.wait_ge(lnx_step, 3 * (u + 1))
                dve.scalar_tensor_tensor(buf, psum[u % 4][:, 0:n], 0.0, buf, ALU.max, ALU.add).then_inc(sp_ready, 1)
                dve.wait_ge(sp_ready, 2 * u + 1)
                dve.tensor_tensor(sp[:, u % 2, 0:P], sp[:, u % 2, 0:P], sq_plain[:, MASK, :], ALU.mult).then_inc(sp_ready, 1)
                dve.wait_ge(sp_ready, 2 * u + 2)
                if h >= 2:
                    dve.wait_ge(expo_ready, CT * (h - 1))
                dve.tensor_copy(l_hi[:, h % 2, cols], buf).then_inc(lhi_ready, 1)
                dve.wait_ge(lhi_ready, u + 1)
                dve.tensor_tensor(l_lo[:, h % 2, cols], buf, l_hi[:, h % 2, cols].bitcast(F32), ALU.subtract).then_inc(l_ready, 1)
            split_w(len(UNITS) - 2)
            split_w(len(UNITS) - 1)
            take_o(HEADS - 1)
            for n, t0 in ((8, 0), (9, CT)):
                for k in range(CT):
                    add_square(n, k)
                norm_rest(n, o, t0)
            dve.wait_ge(keys_hi, 1)
            dve.tensor_tensor(key_lo[:, :, :], key32[:, :, :], key_hi[:, :, :].bitcast(F32), ALU.subtract).then_inc(keys_ready, 1)
            g0 = SEG["mix_out"][0]
            for k in range(KT):
                dve.wait_ge(pe_groups, g0 + k + 1)
                dve.tensor_tensor(x[:, k, :], psum[k][:, :], x[:, k, :], ALU.add).then_inc(x_ready, 1)
                if k:
                    add_square(10, k - 1)
            add_square(10, KT - 1)
            norm_rest(10)
            dve.tensor_copy(iota_b[:, :], sq_plain[:, IOTA, :]).then_inc(iota_ready, 1)
            tops = [0]

            def tops_done():
                dve.wait_ge(top_step, tops[0])

            def top(ins):
                tops[0] += 1
                ins.then_inc(top_step, 1)

            def best_keys(t):
                h, half = t // 2, t % 2
                dve.wait_ge(scores_done, t + 1)
                s = [psum[2 + t % 2][:, tt * P:(tt + 1) * P] for tt in range(TT)]
                v, ix = top_v[:, h, half, :, :], top_i[:, h, half, :, :]
                for tt in range(TT):
                    top(dve.max(v[:, tt, 0:8], s[tt]))
                tops_done()
                for tt in range(TT):
                    top(dve.match_replace(rest1[:, tt, :], v[:, tt, 0:8], s[tt], LOWEST))
                    top(dve.max_index(ix[:, tt, 0:8], v[:, tt, 0:8], s[tt]))
                tops_done()
                for tt in range(TT):
                    top(dve.max(v[:, tt, 8:16], rest1[:, tt, :]))
                tops_done()
                for tt in range(TT):
                    top(dve.max_index(ix[:, tt, 8:16], v[:, tt, 8:16], rest1[:, tt, :]))
                assert tops[0] == 5 * TT * (t + 1)

            for t in range(HP + 1):
                if t < HP:
                    dve.wait_ge(qthi_ready, t + 1)
                    dve.tensor_tensor(qt_lo[:, t % 2, :], psum[t % 2][:, :], qt_hi[:, t % 2, :].bitcast(F32), ALU.subtract).then_inc(qt_ready, 1)
                if t:
                    tops_done()
                    best_keys(t - 1)
            tops_done()
            steps = [0]

            def sel(ins):
                steps[0] += 1
                ins.then_inc(sel_step, 1)

            def seld():
                dve.wait_ge(sel_step, steps[0])

            sel(dve.tensor_copy(top_b[:, :, :, :, :], top_i[:, :, :, :, :]))
            dve.wait_ge(iota_ready, 1)

            def best_pairs(tt):
                grid = [P, PH, TOP, TOP]
                seld()
                sel(dve.tensor_tensor(cand[:, :, :].rearrange("p h (a b) -> p h a b", a=TOP),
                                      top_v[:, :, 0, tt, :].unsqueeze(3).to_broadcast(grid),
                                      top_v[:, :, 1, tt, :].unsqueeze(2).to_broadcast(grid), ALU.add))
                seld()
                for h in range(PH):
                    sel(dve.max(best_v[:, h, 0:8], cand[:, h, :]))
                seld()
                for h in range(PH):
                    sel(dve.match_replace(rest2[:, h, :], best_v[:, h, 0:8], cand[:, h, :], LOWEST))
                    sel(dve.max_index(best_p[:, h, 0:8], best_v[:, h, 0:8], cand[:, h, :]))
                seld()
                for h in range(PH):
                    sel(dve.max(best_v[:, h, 8:16], rest2[:, h, :]))
                seld()
                dve.tensor_tensor(below[:, :, :], best_v[:, :, :], best_v[:, :, 0:1].to_broadcast([P, PH, TOP]), ALU.subtract).then_inc(below_ready, 1)
                for h in range(PH):
                    sel(dve.max_index(best_p[:, h, 8:16], best_v[:, h, 8:16], rest2[:, h, :]))
                seld()
                sel(dve.tensor_scalar(pos_u[:, 0, :, :], best_p[:, :, :], 4, None, ALU.logical_shift_right))
                sel(dve.tensor_scalar(pos_u[:, 1, :, :], best_p[:, :, :], 15, None, ALU.bitwise_and))
                seld()
                sel(dve.tensor_copy(pos_b[:, :, :, :], pos_u[:, :, :, :]))
                seld()
                for half in range(2):
                    sel(dve.tensor_tensor(is_pos[:, :, :, :], iota_b[:, 0:TOP].unsqueeze(1).unsqueeze(1).to_broadcast(grid),
                                          pos_b[:, half, :, :].unsqueeze(3).to_broadcast(grid), ALU.is_equal))
                    seld()
                    sel(dve.tensor_tensor(prod[:, :, :, :], is_pos[:, :, :, :],
                                          top_b[:, :, half, tt, :].unsqueeze(2).to_broadcast(grid), ALU.mult))
                    seld()
                    if half == 0 and tt:
                        dve.wait_ge(turned, tt)
                    sel(dve.tensor_reduce(chosen[:, half, :].rearrange("p (h r) -> p h r", h=PH), prod[:, :, :, :], AXX, ALU.add))
                    seld()
                dve.wait_ge(exp_ready, tt + 1)
                sel(dve.tensor_reduce(esum[:, 0, :], expo[:, :, :], AXX, ALU.add))
                seld()
                sel(dve.reciprocal(esum[:, 1, :], esum[:, 0, :]))
                seld()
                dve.tensor_tensor(chosen[:, 2, :].rearrange("p (h r) -> p h r", h=PH), expo[:, :, :],
                                  esum[:, 1, :].unsqueeze(2).to_broadcast([P, PH, TOP]), ALU.mult).then_inc(chosen_ready, 1)

            picks = [0]

            def pk(ins):
                picks[0] += 1
                ins.then_inc(pick_step, 1)
                dve.wait_ge(pick_step, picks[0])

            def take_turned(tt):
                cols = slice(tt * P, (tt + 1) * P)
                dve.wait_ge(turned, tt + 1)
                w = psum[0][:, 2 * P:3 * P]
                pk(dve.tensor_copy(pick[:, 0:2, cols], psum[0][:, 0:2 * P].rearrange("p (a t) -> p a t", a=2)))
                pk(dve.tensor_copy(pick[:, 2, cols], w))
                pk(dve.tensor_tensor(left[:, 0, :], w, pick[:, 2, cols], ALU.subtract))
                pk(dve.tensor_copy(pick[:, 3, cols], left[:, 0, :]))
                pk(dve.tensor_tensor(left[:, 1, :], left[:, 0, :], pick[:, 3, cols], ALU.subtract))
                pk(dve.tensor_copy(pick[:, 4, cols], left[:, 1, :]))

            for tt in range(TT):
                best_pairs(tt)
                take_turned(tt)
            def rows(c, i):
                s = c % 2
                if c >= 2:
                    dve.wait_ge(hot_used, at(c - 1, i, 4))
                    dve.wait_ge(hot_third, at(c - 1, i, 4))
                numbers = iota_b[:, :].unsqueeze(1).to_broadcast([P, TC, P])
                dve.tensor_tensor(hot_m[:, s, :, :], numbers, hot_column(1, c, i), ALU.is_equal).then_inc(hot_mark, 1)
                dve.tensor_tensor(hot_n[:, s, :, :], numbers, hot_column(0, c, i), ALU.is_equal).then_inc(hot_ready, 1)
                dve.wait_ge(hot_mark, at(c + 1, i, 4))
                for part in range(2):
                    dve.tensor_tensor(hot_w[:, s, part, :, :], hot_m[:, s, :, :], hot_column(2 + part, c, i), ALU.mult).then_inc(hot_ready, 1)

            for c in range(4):
                rows(c, None)
            with dve.Fori(0, T // TC // 4 - 1) as i:
                for c in range(4, 8):
                    rows(c, i)
            def out_step(b, i):
                for j in range(MB):
                    m = MB * b + j
                    if b < NB:
                        dve.wait_ge(g_landed[m % 4], at(16 * (m // 4 + 1), i, 16 * 2 * MB // 4))
                        dve.wait_ge(a_landed[m % 4], at(16 * (m // 4 + 1), i, 16 * 2 * MB // 4))
                        if m >= 2:
                            dve.wait_ge(we_ready, at(m - 1, i, 2 * MB))
                        dve.tensor_tensor(we32[:, m % 2, :], act_in[:, m % 4, :], g_ring[:, m % 4, :], ALU.mult).then_inc(we_mul, 1)
                        dve.wait_ge(we_hi_ready, at(m + 1, i, 2 * MB))
                        if b >= 2 and j == 0:
                            dve.wait_ge(pe_groups, at(v_group(b - 2, KT - 1) + 1, i, 2 * MB))
                        dve.tensor_tensor(we[:, b % 2, 1, j, :], we32[:, m % 2, :], we[:, b % 2, 0, j, :].bitcast(F32),
                                          ALU.subtract).then_inc(we_ready, 1)
                    if b:
                        dve.wait_ge(pe_groups, at(v_group(b - 1, j) + 1, i, 2 * MB))
                        if b >= 2:
                            dve.wait_ge(y_added, at(KT * (b - 2) + j + 1, i, 2 * KT))
                        dve.tensor_tensor(x[:, j, :], psum[j][:, :], x[:, j, :], ALU.add).then_inc(y_added, 1)

            out_step(0, None)
            out_step(1, None)
            with dve.Fori(0, NB // 2 - 1) as i:
                out_step(2, i)
                out_step(3, i)
            out_step(NB, None)

        @block.tensor
        def _(pe):
            def three(bank, s, b, rhi, rlo, start, stop, last=None):
                pe.matmul(bank, whi[:, s, b, :], rhi, start=start, stop=False)
                pe.matmul(bank, whi[:, s, b, :], rlo, start=False, stop=False)
                return pe.matmul(bank, wlo[:, s, b, :], rhi, start=False, stop=stop)

            def row_group(bank, c, i=None, m=0, hi=None, lo=None, first=None, ready=h_ready):
                hi = hhi if hi is None else hi
                lo = hlo if lo is None else lo
                pe.wait_ge(lo_ready, at(c + 1, i, m))
                for k in range(GB):
                    if first is not None:
                        pe.wait_ge(ready, first + k + 1)
                    mm = three(bank, c % R, k, hi[:, k, :], lo[:, k, :], k == 0, k == GB - 1)
                mm.then_inc(pe_groups, 1)

            def first_pair(banks, c, first):
                pe.wait_ge(lo_ready, c + 2)
                for k in range(GB):
                    pe.wait_ge(hhi_ready, first + k + 1)
                    for g in range(2):
                        s = (c + g) % R
                        pe.matmul(banks[g][:, :], whi[:, s, k, :], hhi[:, k, :], start=k == 0, stop=False)
                        pe.matmul(banks[g][:, :], wlo[:, s, k, :], hhi[:, k, :], start=False, stop=False)
                for k in range(GB):
                    pe.wait_ge(h_ready, first + k + 1)
                    for g in range(2):
                        mm = pe.matmul(banks[g][:, :], whi[:, (c + g) % R, k, :], hlo[:, k, :], start=False, stop=k == GB - 1)
                        if k == GB - 1:
                            mm.then_inc(pe_groups, 1)

            def ada_sums(it, i=None, m=0):
                pe.wait_ge(ada_used, at(16 * (it + 1), i, 16 * m))
                if it:
                    pe.wait_ge(mod_ready, at(it, i, m))
                for c in range(KT):
                    acc = ada_accs[c // 4]
                    mm = pe.matmul(psum[6][:, c:c + 1], acc[:, (c % 4) * P:(c % 4 + 1) * P], one_col[:, :], start=True, stop=True)
                mm.then_inc(ada_summed, 1)

            def mean_square(n):
                pe.wait_ge(sq_used, tiles_before(ALL_NORMS, n) + NORM_TILES[n])
                weights = sq_plain[:, MEAN_H, :] if n in (8, 9) else mean_d[:, :]
                pe.matmul(psum[7][:, :], weights, sqsum[:, :], start=True, stop=True).then_inc(ms_ready, 1)

            def ffn(q, h_first):
                g0 = SEG[f"ffn{q}_in"][0]
                it0 = ADA_AT.get(q)

                def tile(j, i):
                    t = FT * q + j
                    if j >= 2:
                        pe.wait_ge(u_mul, at(t - 1, i, BODY))
                    row_group(psum[2 * (j % 2)][:, :], g0 + 2 * j, i, 2 * BODY)
                    row_group(psum[2 * (j % 2) + 1][:, :], g0 + 2 * j + 1, i, 2 * BODY)

                first_pair(psum[0:2], g0, h_first)
                for j in range(1, BODY):
                    tile(j, None)
                with pe.Fori(0, BODIES - 1) as i:
                    for j in range(BODY, 2 * BODY):
                        tile(j, i)
                        if j == BODY and it0 is not None:
                            ada_sums(it0, i, 1)
                for j in range(BODY * BODIES, FT):
                    tile(j, None)
                    if j == BODY * BODIES and it0 is not None:
                        ada_sums(it0 + BODIES - 1)
                if it0 is not None:
                    pe.wait_ge(mod_ready, it0 + BODIES)
                g1 = SEG[f"ffn{q}_out"][0]

                def out_group(half, f, i):
                    c = g1 + half * (FT // 2) + f
                    pe.wait_ge(lo_ready, at(c + 1, i, 4))
                    pe.wait_ge(u_ready, at(FT * q + 2 * f + 2, i, 8))
                    last = i is None and f == FT // 2 - 1
                    if i is None:
                        tiles = [(uhi[:, 2 * f + a, :], ulo[:, 2 * f + a, :]) for a in range(2)]
                    else:
                        tiles = [[z[:, bass.ds(i * 8 + 2 * f + a, 1), :].rearrange("p a t -> p (a t)") for z in (uhi, ulo)] for a in range(2)]
                    for d in range(4):
                        for a in range(2):
                            mm = three(psum[4 - 4 * half + d][:, :], c % R, a * 4 + d, *tiles[a],
                                       f == 0 and a == 0, last and a == 1)
                        if last and d < 3:
                            mm.then_inc(bank_done, 1)
                    mm.then_inc(pe_groups, 1)

                for half in range(2):
                    if half:
                        pe.wait_ge(u_mul, FT * (q + 1))
                    out_group(half, 0, None)
                    with pe.Fori(0, 2) as i:
                        for f in range(1, 5):
                            out_group(half, f, i)
                    out_group(half, 9, None)
                    out_group(half, 10, None)

            pe.wait_ge(const_landed, 64)
            pe.wait_ge(setup_done, 1)
            mean_square(0)
            pe.wait_ge(ada_used, 32)
            for c in range(2 * KT):
                mm = pe.matmul(psum[6][:, c:c + 1], first_acc[:, c * P:(c + 1) * P], one_col[:, :], start=True, stop=True)
            mm.then_inc(ada_summed, 2)
            ffn(0, 0)
            ada_sums(LATE)
            mean_square(1)
            for g in range(4):
                c = SEG["pool"][0] + g // 2
                if g % 2 == 0:
                    pe.wait_ge(lo_ready, c + 1)
                pe.wait_ge(pool_ready, 2 * g + 2)
                for o in range(2):
                    for k in range(2):
                        mm = three(psum[2 * g + o][:, :], c % R, (g % 2) * 4 + o * 2 + k, hhi[:, 2 * g + k, :], hlo[:, 2 * g + k, :],
                                   k == 0, k == 1)
                if g % 2:
                    mm.then_inc(pe_groups, 1)
            mean_square(2)
            ffn(1, KT)
            mean_square(3)
            ffn(2, 2 * KT)
            mean_square(4)
            g0 = SEG["conv_in"][0]
            first_pair(psum[0:2], g0, 3 * KT)
            for j in range(KT):
                for part in range(2 if j == 0 else 0, 3):
                    if j >= 2 and part == 0:
                        pe.wait_ge(y32_ready, j - 1)
                    row_group(psum[3 * (j % 2) + part][:, :], g0 + 3 * j + part)
            g0 = SEG["conv_out"][0]
            for k in range(KT):
                row_group(psum[k][:, :], g0 + k, hi=yhi, lo=ylo, first=0 if k == 0 else None, ready=y_ready)
            mean_square(5)
            ffn(3, 4 * KT)
            mean_square(6)
            mean_square(7)
            g0 = SEG["xr"][0]
            first_pair(psum[0:2], g0, 5 * KT)
            for c in range(2, CT):
                row_group(psum[c][:, :], g0 + c)
            g0 = SEG["qk"][0]

            def q_mean(t):
                pe.wait_ge(qsq_ready, t + 1)
                if t >= 2:
                    pe.wait_ge(qstd_ready, t - 1)
                pe.matmul(psum[6 + t % 2][:, :], sq_plain[:, BLK, :], qsq[:, t % 2, :], start=True, stop=True).then_inc(qms_ready, 1)

            for t in range(2 * CT):
                if t >= 4:
                    pe.wait_ge(qn_ready, t - 3)
                elif t >= 2:
                    pe.wait_ge(xpad_ready, t + 1)
                row_group(psum[QK_BANK[t % 4]][:, :], g0 + t)
                if t:
                    q_mean(t - 1)
            q_mean(2 * CT - 1)
            c0 = SEG["gates"][0]
            pe.wait_ge(lo_ready, c0 + 1)
            for c in range(CT):
                if c == 1:
                    pe.wait_ge(qn_ready, 2 * CT)
                pe.wait_ge(xc_lo_ready, c + 1)
                if c >= 2:
                    pe.wait_ge(gates_ready, 2 * c - 2)
                for part in range(2):
                    mm = three(psum[2 * (c % 2) + part][:, :], c0 % R, 2 * c + part, xc_hi[:, c, :], xc_lo[:, c, :], True, True)
                mm.then_inc(gate_products if c < CT - 1 else pe_groups, 1)
            g0 = SEG["gr"][0]
            pe.wait_ge(qn_ready, 2 * CT)
            for c in range(CT):
                row_group(psum[4 + c][:, :], g0 + c)
            g0 = SEG["v"][0]
            pe.wait_ge(gates_ready, 2 * CT)
            for c in range(CT):
                s = (g0 + c) % R
                pe.wait_ge(lo_ready, g0 + c + 1)
                for a in range(2):
                    k = 2 * c + a
                    rh, rl = (w[:, s, 4 * a:4 * a + 4, :].rearrange("p b n -> p (b n)") for w in (whi, wlo))
                    for st in range(CT):
                        cols = slice(st * P, st * P + P)
                        pe.matmul(psum[st][:, :], hhi[:, k, cols], rh, start=k == 0, stop=False)
                        pe.matmul(psum[st][:, :], hlo[:, k, cols], rh, start=False, stop=False)
                        mm = pe.matmul(psum[st][:, :], hhi[:, k, cols], rl, start=False, stop=k == KT - 1)
                mm.then_inc(pe_groups, 1)
            def scores(u):
                h, i = UNITS[u]
                n = T - P * i
                if u >= 4:
                    pe.wait_ge(w32_ready, u - 3)
                r, t = slice(64 * (h % 2), 64 * (h % 2) + 64), h // 2
                out = psum[u % 4][:, 0:n]
                kc, qc = slice(P * i, P * i + P), slice(P * i, T)
                pe.matmul(out, k_hi[r, t, kc], q_hi[r, t, qc], start=True, stop=False)
                pe.matmul(out, k_hi[r, t, kc], q_lo[r, t, qc], start=False, stop=False)
                pe.matmul(out, k_lo[r, t, kc], q_hi[r, t, qc], start=False, stop=True).then_inc(z_ready, 1)

            def exponent(u):
                h, i = UNITS[u]
                pe.wait_ge(l_ready, u + 1)
                for j in range(i, CT):
                    off = P * (j - i)
                    n = T - P * j
                    out = psum[u % 4][:, off:off + n]
                    for part in (l_hi, l_lo):
                        pe.matmul(out, sq_round[:, TRI if j == i else ONES, :], part[:, h % 2, ATT_OFF[j]:ATT_OFF[j] + n],
                                  start=False, stop=False, skip_group_check=True)
                pe.matmul(psum[u % 4][:, 0:P], sq_round[:, IDENT_R, :], sq_round[:, FAR, :],
                          start=False, stop=True, skip_group_check=True).then_inc(expo_ready, 1)

            def weighted(u):
                h, i = UNITS[u]
                n = T - P * i
                pe.wait_ge(w_ready, u + 1)
                if i == CT - 1 and h >= 2:
                    pe.wait_ge(o_ready, h - 1)
                out = psum[4 + h % 2][:, P * i:T]
                fc = slice(P * (h // 2), P * (h // 2) + P)
                pe.matmul(out, v_hi[:, i, fc], w_hi[:, u % 2, 0:n], start=i == CT - 1, stop=False, skip_group_check=True)
                pe.matmul(out, v_hi[:, i, fc], w_lo[:, u % 2, 0:n], start=False, stop=False, skip_group_check=True)
                pe.matmul(out, v_lo[:, i, fc], w_hi[:, u % 2, 0:n], start=False, stop=i == 0, skip_group_check=True).then_inc(pv_done, 1)

            pe.wait_ge(q_ready, 2 * CT)
            pe.wait_ge(const2_ready, 1)
            pe.wait_ge(v_ready, CT)
            pe.wait_ge(rg_out, CT)
            for u in range(len(UNITS) + 3):
                if u < len(UNITS):
                    scores(u)
                if 2 <= u < len(UNITS) + 2:
                    exponent(u - 2)
                if u >= 3:
                    weighted(u - 3)
            mean_square(8)
            mean_square(9)
            g0 = SEG["mix_out"][0]
            first_pair(psum[0:2], g0, tiles_before(SPLIT_NORMS, 8))
            for k in range(2, KT):
                row_group(psum[k][:, :], g0 + k)
            mean_square(10)

            def keyed_scores(t):
                pe.wait_ge(qt_ready, t + 1)
                if t >= 2:
                    pe.wait_ge(top_step, 5 * TT * (t - 1))
                for tt in range(TT):
                    cols = slice(tt * P, (tt + 1) * P)
                    out = psum[2 + t % 2][:, cols]
                    pe.matmul(out, qt_hi[:, t % 2, cols], key_hi[:, t, :], start=True, stop=False)
                    pe.matmul(out, qt_hi[:, t % 2, cols], key_lo[:, t, :], start=False, stop=False)
                    mm = pe.matmul(out, qt_lo[:, t % 2, cols], key_hi[:, t, :], start=False, stop=True)
                mm.then_inc(scores_done, 1)

            g0 = SEG["query"][0]
            pe.wait_ge(keys_ready, 1)
            first_pair(psum[0:2], g0, tiles_before(SPLIT_NORMS, 10))
            for t in range(HP + 1):
                if 2 <= t < HP:
                    pe.wait_ge(qt_ready, t - 1)
                    row_group(psum[t % 2][:, :], g0 + t)
                if t:
                    keyed_scores(t - 1)
            up = SEG["up"][0]

            def column(m, i):
                if m >= 4:
                    pe.wait_ge(gelu_done, at(m - 3, i, 4))
                row_group(psum[4 + m % 4][:, :], up + m, i, 4)

            def columns_run(m0, n):
                if m0 == 0:
                    for m in range(4):
                        column(m, None)
                    m0, n = 4, n - 4
                with pe.Fori(0, n // 4) as i:
                    for m in range(m0, m0 + 4):
                        column(m, i)

            def sums(c, i):
                s = c % 2
                pe.wait_ge(hot_ready, at(3 * (c + 1), i, 12))
                pe.wait_ge(hot_third, at(c + 1, i, 4))
                if c >= 2:
                    pe.wait_ge(spread_ready, at(2 * (c - 1), i, 8))
                for k in range(TC):
                    out = psum[2 * s + k // 4][:, (k % 4) * P:(k % 4 + 1) * P]
                    for part in range(3):
                        mm = pe.matmul(out, hot_n[:, s, k, :], hot_w[:, s, part, k, :], start=part == 0, stop=part == 2)
                mm.then_inc(hot_used, 1)

            for tt in range(TT):
                columns_run(tt * LEAD, LEAD)
                pe.wait_ge(chosen_ready, tt + 1)
                if tt:
                    pe.wait_ge(pick_step, 6 * tt)
                for part in range(3):
                    mm = pe.matmul(psum[0][:, part * P:(part + 1) * P], chosen[:, part, :], sq_plain[:, IDENT, :], start=True, stop=True)
                mm.then_inc(turned, 1)
            for tt in range(TT):
                m0 = TT * LEAD + tt * (CHUNKS + GAP)
                c0 = tt * CHUNKS
                if tt == 0:
                    for k in range(4):
                        column(m0 + k, None)
                        sums(c0 + k, None)
                    m0, c0 = m0 + 4, c0 + 4
                with pe.Fori(0, CHUNKS // 4 - (tt == 0)) as i:
                    for k in range(4):
                        column(m0 + k, i)
                        sums(c0 + k, i)
                columns_run(TT * LEAD + tt * (CHUNKS + GAP) + CHUNKS, GAP)
            def down(b, i):
                pe.wait_ge(we_ready, at(MB * (b + 1), i, 2 * MB))
                for d in range(KT):
                    if b:
                        pe.wait_ge(y_added, at(KT * (b - 1) + d + 1, i, 2 * KT))
                    row_group(psum[d][:, :], v_group(b, d), i, 2 * MB,
                              hi=we[:, b % 2, 0, :, :], lo=we[:, b % 2, 1, :, :])

            pe.wait_ge(spread_ready, 2 * T // TC)
            pe.wait_ge(gelu_done, NK)
            down(0, None)
            down(1, None)
            with pe.Fori(0, NB // 2 - 1) as i:
                down(2, i)
                down(3, i)


def columns(v):
    return np.ascontiguousarray(np.asarray(v).reshape(-1, P).T)


def rows_as_groups(w):
    w = np.asarray(w)
    n = w.shape[1] // P
    return w.reshape(KT, P, n, P).transpose(2, 1, 0, 3)


def layout(x, c, ada_w, ada_b, norm_g, ffn_w_in, ffn_w_out, pool_w, pool_scale, conv_w_in, conv_w, conv_w_out, final_g,
           norm_mix_2, w_in_2, q_norm_2, k_norm_2, conv_w_2, conv_b_2, rg_w_a_2, rg_b_a_2, rg_w_x_2, rg_b_x_2, rg_lambda_2,
           out_norm_sb_2, out_norm_rg_2, w_out_2, norm_ffn_2, peer_w_query_2, peer_sub_keys_2, peer_u_2, peer_v_2):
    A = np.asarray
    parts = []

    def ffn(l, s):
        g = rows_as_groups(A(ffn_w_in)[l, s])
        parts.append(np.stack([g[:FT], g[FT:]], 1).reshape(2 * FT, P, GB, P))
        w = A(ffn_w_out)[l, s].reshape(FT // 2, 2, P, 2, 4, P)
        parts.append(w.transpose(3, 0, 2, 1, 4, 5).reshape(FT, P, GB, P))

    ffn(0, 0)
    pw = A(pool_w)[0].reshape(2, 2, 2, P, 2, P)
    parts.append(pw.transpose(0, 3, 1, 4, 2, 5).reshape(2, P, GB, P))
    ffn(0, 1)
    ffn(1, 0)
    g = rows_as_groups(A(conv_w_in)[0])
    parts.append(np.stack([g[8:16], g[16:24], g[0:8]], 1).reshape(24, P, GB, P))
    parts.append(rows_as_groups(A(conv_w_out)[0]))
    ffn(1, 1)
    g = rows_as_groups(A(w_in_2)[0])
    parts.append(g[12:16])
    parts.append(g[0:8])
    gates = np.zeros((1, P, GB, P), np.float32)
    for b in range(8):
        for part, w in enumerate((rg_w_a_2, rg_w_x_2)):
            r = slice(64 * (b % 2), 64 * (b % 2) + 64)
            gates[0, r, 2 * (b // 2) + part, r] = A(w)[0, b]
    parts.append(gates)
    parts.append(g[16:20])
    v = A(w_in_2)[0][:, 1024:1536].reshape(4, 2, P, 4, P)
    parts.append(v.transpose(0, 2, 1, 3, 4).reshape(4, P, GB, P))
    parts.append(rows_as_groups(A(w_out_2)[0]))
    parts.append(rows_as_groups(A(peer_w_query_2)[0].reshape(D, HP * P)))
    u = A(peer_u_2)[0].reshape(NK, NK, KT, P).transpose(1, 3, 2, 0)
    v = A(peer_v_2)[0].reshape(NK, NB, MB, KT, P).transpose(1, 3, 0, 2, 4).reshape(NB, KT, P, GB, P)
    parts.append(u)
    parts.append(v.reshape(NK, P, GB, P))
    sub_keys = np.ascontiguousarray(A(peer_sub_keys_2)[0].reshape(HP, NK, P).transpose(2, 0, 1))
    stream = np.concatenate(parts)
    ada = A(ada_w).reshape(2 * KT, P, 9 * D)
    smalls = np.concatenate([columns(A(c)), columns(A(ada_b)), columns(A(norm_g)), columns(A(pool_scale)), columns(A(conv_w)),
                             columns(A(final_g)), np.zeros((P, KT), np.float32), np.full((P, 1), 1e-6, np.float32)], 1)
    corr = np.concatenate([w / np.arange(1, w) for w in (2, 4, 8, 16)] + [np.zeros(6)])
    consts = np.concatenate([np.full((P, P), 1 / D), np.tile(corr, (P, 1))], 1).astype(np.float32)
    xin = np.ascontiguousarray(A(x)[0].T.reshape(KT, P, T).transpose(1, 0, 2))
    twice = lambda g: np.tile(A(g).reshape(64, 1), (2, 1))
    smalls2 = np.concatenate([columns(A(norm_mix_2)), twice(q_norm_2), twice(k_norm_2), columns(A(conv_w_2)), columns(A(conv_b_2)),
                              columns(A(rg_b_a_2)), columns(A(rg_b_x_2)), columns(A(rg_lambda_2)),
                              columns(A(out_norm_sb_2)), columns(A(out_norm_rg_2)), columns(A(norm_ffn_2)),
                              np.zeros((P, KT), np.float32), np.full((P, 1), 1e-6, np.float32)], 1)
    r = np.arange(P)
    key, query = r[:, None], r[None, :]
    consts2 = np.stack([(key // 64 == query // 64) / 64.0, key < query, np.full((P, P), 1 / 512), key == query, np.tile(r, (P, 1)),
                        -1.0 * (key >= query), -np.ones((P, P)), key == query, np.where(key < query, 0.0, -1e30)], 1).astype(np.float32)
    return {"stream": stream, "ada": ada, "smalls": smalls, "consts": consts, "smalls2": smalls2, "consts2": consts2,
            "keys": sub_keys, "xin": xin}


def kernel(**inputs):
    import concourse.bacc as bacc
    from concourse.bass_utils import run_bass_kernel_spmd

    nc = bacc.Bacc("TRN2", target_bir_lowering=False, num_devices=1)
    arrays, args = {}, []
    for name, a in layout(**inputs).items():
        arrays[name + "_dram"] = a
        args.append(nc.dram_tensor(name + "_dram", a.shape, mybir.dt.from_np(a.dtype), kind="ExternalInput").ap())
    args.append(nc.dram_tensor("out_dram", (P, KT, T), F32, kind="ExternalOutput").ap())
    build(nc, *args)
    r = run_bass_kernel_spmd(nc, [arrays], core_ids=[0])
    y = r.results[0]["out_dram"]
    return np.ascontiguousarray(y.transpose(2, 1, 0).reshape(1, T, D))
```
